# Optimizing a Trainium2 kernel written in Bass

```python
import math
import jax, jax.numpy as jnp
from jax import lax
import numpy as np

D_MODEL = 1024
BATCH = 1
SEQ = 256
DEPTH = 2
DEC_BATCH = 8
DEC_SEQ = 1
PAST_LEN = 2048
PAGE_SIZE = 128

POOL_WIDTH = D_MODEL // 2
POOL_WINDOWS = (2, 4, 8, 16)
N_POOL_GROUPS = len(POOL_WINDOWS)
POOL_GROUP = POOL_WIDTH // N_POOL_GROUPS
POOL_STATE = max(POOL_WINDOWS) - 1
SSM_WIDTH = D_MODEL // 2
SSM_GROUP = 16
N_SSM_GROUPS = SSM_WIDTH // SSM_GROUP
SSM_STATE = 64
DT_MIN = 1e-3
DT_MAX = 1e-1
IN_WIDTH = POOL_WIDTH + SSM_WIDTH + 2 * D_MODEL
D_FF = 11 * D_MODEL // 4
N_EXPERTS = 8
TOP_K = 2
D_FF_EXPERT = 7 * D_MODEL // 2
N_DENSE = (DEPTH + 1) // 2
N_MOE = DEPTH // 2
ALPHA = (2.0 * DEPTH) ** 0.25
BETA = (8.0 * DEPTH) ** -0.25
LN_EPS = 1e-5

kernel_name = "hybrid_pool_s5_deepnorm_moe_step"

def layer_norm(x, g, b):
    xf = x.astype(jnp.float32)
    mu = jnp.mean(xf, axis=-1, keepdims=True)
    var = jnp.mean(jnp.square(xf - mu), axis=-1, keepdims=True)
    y = (xf - mu) * lax.rsqrt(var + LN_EPS) * g.astype(jnp.float32) + b.astype(jnp.float32)
    return y.astype(x.dtype)

def pool_mixer(u, prev, start_pos, w_pool, pool_scale):
    L = u.shape[1]
    u_ext = jnp.concatenate([prev.astype(u.dtype), u], axis=1)
    cs = jnp.cumsum(u_ext.astype(jnp.float32), axis=1)
    cs = jnp.concatenate([jnp.zeros_like(cs[:, :1]), cs], axis=1)
    hi = cs[:, POOL_STATE + 1:]
    uf = u.astype(jnp.float32)
    pos = start_pos + jnp.arange(L)
    groups = []
    for gi, w in enumerate(POOL_WINDOWS):
        sl = slice(gi * POOL_GROUP, (gi + 1) * POOL_GROUP)
        lo = cs[:, POOL_STATE + 1 - w: POOL_STATE + 1 - w + L, sl]
        count = jnp.minimum(w, pos + 1).astype(jnp.float32)[None, :, None]
        groups.append((hi[..., sl] - lo) / count - uf[..., sl])
    pooled = jnp.stack(groups, axis=2).astype(u.dtype)
    mixed = jnp.einsum('blgc,gcd->blgd', pooled, w_pool)
    out = mixed.reshape(u.shape) * pool_scale
    return out, u_ext[:, -POOL_STATE:]

def ssm_mixer(u, h0_re, h0_im, lambda_re, lambda_im, log_dt, b_re, b_im, c_re, c_im, d_skip, w_glu, b_glu):
    f32 = jnp.float32
    bsz, L, _ = u.shape
    uf = u.astype(f32).reshape(bsz, L, N_SSM_GROUPS, SSM_GROUP)
    lam = lax.complex(lambda_re.astype(f32), lambda_im.astype(f32))
    dt = jnp.exp(log_dt.astype(f32))[:, None]
    lam_bar = jnp.exp(lam * dt)
    b_mat = lax.complex(b_re.astype(f32), b_im.astype(f32))
    b_bar = ((lam_bar - 1.0) / lam)[..., None] * b_mat
    bu = jnp.einsum('blgc,gpc->blgp', uf.astype(jnp.complex64), b_bar)
    h0 = lax.complex(h0_re.astype(f32), h0_im.astype(f32))
    bu = bu.at[:, 0].add(lam_bar * h0)
    a = jnp.broadcast_to(lam_bar, bu.shape)

    def combine(left, right):
        a_l, b_l = left
        a_r, b_r = right
        return a_l * a_r, a_r * b_l + b_r

    _, h = lax.associative_scan(combine, (a, bu), axis=1)
    c_mat = lax.complex(c_re.astype(f32), c_im.astype(f32))
    y = jnp.real(jnp.einsum('blgp,gcp->blgc', h, c_mat)) + d_skip.astype(f32) * uf
    y = jax.nn.gelu(y.reshape(bsz, L, SSM_WIDTH)).astype(u.dtype)
    out = y * jax.nn.sigmoid(y @ w_glu + b_glu)
    h_last = h[:, -1]
    return out, jnp.real(h_last), jnp.imag(h_last)

def token_mix(x, pool_prev, h0_re, h0_im, start_pos, p):
    z = x @ p['w_in'] + p['b_in']
    u_a, u_b, z_ga, z_gb = jnp.split(
        z, [POOL_WIDTH, POOL_WIDTH + SSM_WIDTH, POOL_WIDTH + SSM_WIDTH + D_MODEL], axis=-1)
    out_a, pool_new = pool_mixer(u_a, pool_prev, start_pos, p['w_pool'], p['pool_scale'])
    out_b, h_re, h_im = ssm_mixer(u_b, h0_re, h0_im, p['lambda_re'], p['lambda_im'], p['log_dt'],
                                  p['b_re'], p['b_im'], p['c_re'], p['c_im'], p['d_skip'],
                                  p['w_glu'], p['b_glu'])
    merged = (jax.nn.sigmoid(z_ga) * (out_a @ p['w_proj_a'])
              + jax.nn.sigmoid(z_gb) * (out_b.astype(x.dtype) @ p['w_proj_b']))
    return merged @ p['w_out'], pool_new, h_re, h_im

def swiglu(x, wg, wu, wd):
    return (jax.nn.silu(x @ wg) * (x @ wu)) @ wd

def moe_swiglu(x, w_router, b_router, wg, wu, wd):
    f32 = jnp.float32
    logits = x.astype(f32) @ w_router.astype(f32) + b_router.astype(f32)
    top_val, top_idx = lax.top_k(logits, TOP_K)
    top_w = jax.nn.softmax(top_val, axis=-1)
    gates = jnp.einsum('blk,blke->ble', top_w, jax.nn.one_hot(top_idx, N_EXPERTS, dtype=f32))
    out = jnp.zeros(x.shape, f32)
    for e in range(N_EXPERTS):
        out = out + gates[..., e:e + 1] * swiglu(x, wg[e], wu[e], wd[e]).astype(f32)
    return out.astype(x.dtype)

def setup_inputs(seed: int = 0) -> dict:
    key = jax.random.key(seed)
    ks = iter(jax.random.split(key, 40))

    def nrm(shape, scale=1.0):
        return jax.random.normal(next(ks), shape, jnp.float32) * scale

    G, P, c = N_SSM_GROUPS, SSM_STATE, SSM_GROUP
    inp = {}
    inp['x_prompt'] = nrm((BATCH, SEQ, D_MODEL))
    inp['x_sample'] = nrm((DEC_BATCH, DEC_SEQ, D_MODEL))
    inp['state_pool'] = nrm((DEPTH, DEC_BATCH, POOL_STATE, POOL_WIDTH))
    inp['state_ssm_re'] = nrm((DEPTH, DEC_BATCH, G, P), 0.1)
    inp['state_ssm_im'] = nrm((DEPTH, DEC_BATCH, G, P), 0.1)
    inp['ln1_g'] = 1.0 + nrm((DEPTH, D_MODEL), 0.02)
    inp['ln1_b'] = nrm((DEPTH, D_MODEL), 0.02)
    inp['w_in'] = nrm((DEPTH, D_MODEL, IN_WIDTH), D_MODEL ** -0.5)
    inp['b_in'] = nrm((DEPTH, IN_WIDTH), 0.02)
    inp['w_pool'] = nrm((DEPTH, N_POOL_GROUPS, POOL_GROUP, POOL_GROUP), POOL_GROUP ** -0.5)
    inp['pool_scale'] = 1.0 + nrm((DEPTH, POOL_WIDTH), 0.02)
    inp['lambda_re'] = -0.5 + nrm((DEPTH, G, P), 0.01)
    inp['lambda_im'] = math.pi * jnp.arange(P, dtype=jnp.float32) + nrm((DEPTH, G, P), 0.01)
    inp['log_dt'] = jax.random.uniform(next(ks), (DEPTH, G), jnp.float32,
                                       math.log(DT_MIN), math.log(DT_MAX))
    inp['b_re'] = nrm((DEPTH, G, P, c), (2.0 * c) ** -0.5)
    inp['b_im'] = nrm((DEPTH, G, P, c), (2.0 * c) ** -0.5)
    inp['c_re'] = nrm((DEPTH, G, c, P), P ** -0.5)
    inp['c_im'] = nrm((DEPTH, G, c, P), P ** -0.5)
    inp['d_skip'] = nrm((DEPTH, G, c))
    inp['w_glu'] = nrm((DEPTH, SSM_WIDTH, SSM_WIDTH), SSM_WIDTH ** -0.5)
    inp['b_glu'] = nrm((DEPTH, SSM_WIDTH), 0.02)
    inp['w_proj_a'] = nrm((DEPTH, POOL_WIDTH, D_MODEL), POOL_WIDTH ** -0.5)
    inp['w_proj_b'] = nrm((DEPTH, SSM_WIDTH, D_MODEL), SSM_WIDTH ** -0.5)
    inp['w_out'] = nrm((DEPTH, D_MODEL, D_MODEL), BETA * D_MODEL ** -0.5)
    inp['ln2_g'] = 1.0 + nrm((DEPTH, D_MODEL), 0.02)
    inp['ln2_b'] = nrm((DEPTH, D_MODEL), 0.02)
    inp['w_ffn_gate'] = nrm((N_DENSE, D_MODEL, D_FF), D_MODEL ** -0.5)
    inp['w_ffn_up'] = nrm((N_DENSE, D_MODEL, D_FF), D_MODEL ** -0.5)
    inp['w_ffn_down'] = nrm((N_DENSE, D_FF, D_MODEL), BETA * D_FF ** -0.5)
    inp['w_router'] = nrm((N_MOE, D_MODEL, N_EXPERTS), D_MODEL ** -0.5)
    inp['b_router'] = nrm((N_MOE, N_EXPERTS), 0.01)
    inp['w_moe_gate'] = nrm((N_MOE, N_EXPERTS, D_MODEL, D_FF_EXPERT), D_MODEL ** -0.5)
    inp['w_moe_up'] = nrm((N_MOE, N_EXPERTS, D_MODEL, D_FF_EXPERT), D_MODEL ** -0.5)
    inp['w_moe_down'] = nrm((N_MOE, N_EXPERTS, D_FF_EXPERT, D_MODEL), BETA * D_FF_EXPERT ** -0.5)
    return inp

def reference(x_prompt, x_sample, state_pool, state_ssm_re, state_ssm_im,
              ln1_g, ln1_b, w_in, b_in, w_pool, pool_scale, lambda_re, lambda_im, log_dt,
              b_re, b_im, c_re, c_im, d_skip, w_glu, b_glu, w_proj_a, w_proj_b, w_out,
              ln2_g, ln2_b, w_ffn_gate, w_ffn_up, w_ffn_down,
              w_router, b_router, w_moe_gate, w_moe_up, w_moe_down):
    y_p, y_s = x_prompt, x_sample
    bp = x_prompt.shape[0]
    zero_pool = jnp.zeros((bp, POOL_STATE, POOL_WIDTH), x_prompt.dtype)
    zero_h = jnp.zeros((bp, N_SSM_GROUPS, SSM_STATE), jnp.float32)
    pool_p, re_p, im_p, pool_s, re_s, im_s = [], [], [], [], [], []
    for l in range(DEPTH):
        p = dict(w_in=w_in[l], b_in=b_in[l], w_pool=w_pool[l], pool_scale=pool_scale[l],
                 lambda_re=lambda_re[l], lambda_im=lambda_im[l], log_dt=log_dt[l],
                 b_re=b_re[l], b_im=b_im[l], c_re=c_re[l], c_im=c_im[l], d_skip=d_skip[l],
                 w_glu=w_glu[l], b_glu=b_glu[l], w_proj_a=w_proj_a[l], w_proj_b=w_proj_b[l],
                 w_out=w_out[l])
        m_p, np_pool, np_re, np_im = token_mix(y_p, zero_pool, zero_h, zero_h, 0, p)
        m_s, ns_pool, ns_re, ns_im = token_mix(y_s, state_pool[l], state_ssm_re[l],
                                               state_ssm_im[l], PAST_LEN, p)
        pool_p.append(np_pool); re_p.append(np_re); im_p.append(np_im)
        pool_s.append(ns_pool); re_s.append(ns_re); im_s.append(ns_im)
        y_p = layer_norm(ALPHA * y_p + m_p.astype(y_p.dtype), ln1_g[l], ln1_b[l])
        y_s = layer_norm(ALPHA * y_s + m_s.astype(y_s.dtype), ln1_g[l], ln1_b[l])
        j = l // 2
        if l % 2 == 0:
            f_p = swiglu(y_p, w_ffn_gate[j], w_ffn_up[j], w_ffn_down[j])
            f_s = swiglu(y_s, w_ffn_gate[j], w_ffn_up[j], w_ffn_down[j])
        else:
            f_p = moe_swiglu(y_p, w_router[j], b_router[j], w_moe_gate[j], w_moe_up[j], w_moe_down[j])
            f_s = moe_swiglu(y_s, w_router[j], b_router[j], w_moe_gate[j], w_moe_up[j], w_moe_down[j])
        y_p = layer_norm(ALPHA * y_p + f_p.astype(y_p.dtype), ln2_g[l], ln2_b[l])
        y_s = layer_norm(ALPHA * y_s + f_s.astype(y_s.dtype), ln2_g[l], ln2_b[l])
    return (y_p, y_s, jnp.stack(pool_p), jnp.stack(re_p), jnp.stack(im_p),
            jnp.stack(pool_s), jnp.stack(re_s), jnp.stack(im_s))


_drawn_inputs = setup_inputs


def setup_inputs(seed=0):
    import zlib

    import numpy as np

    out = dict(_drawn_inputs(seed))
    spreads = {}
    factors = {'pool_scale': 6.97,
     'lambda_re': 17.967,
     'c_re': 4.326,
     'b_glu': 64.0,
     'b_router': 14.04,
     'c_im': 8.0}
    for name, (base, spread) in spreads.items():
        noise = np.random.default_rng([zlib.crc32(name.encode()), seed]).standard_normal(out[name].shape)
        drawn = base * np.exp(spread * noise) if base else spread * noise
        out[name] = __import__('jax').numpy.asarray(drawn.astype(out[name].dtype))
    for name, factor in factors.items():
        out[name] = (out[name] * factor).astype(out[name].dtype)
    return out
```

```python
import math
from contextlib import ExitStack

import concourse.bass as bass
from concourse import mybir

F32 = mybir.dt.float32
I32 = mybir.dt.int32
ALU = mybir.AluOpType
ACT = mybir.ActivationFunctionType
AX = mybir.AxisListType

P = 128
D = 1024
KD = D // P
SEQ = 256
NDEC = 8
T = SEQ + NDEC
TILES = ((0, P), (P, P), (2 * P, NDEC))
DEPTH = 2
CHUNK = 8
NCH = SEQ // CHUNK
UC = NCH + NDEC
PW = 512
WINDOWS = (2, 4, 8, 16)
PSTATE = max(WINDOWS) - 1
PAD = PSTATE + 1
SW = 512
NG = 32
GC = SW // NG
NS = 64
NQ = NG * NS // P
NPOW = CHUNK + 1
FF = 11 * D // 4
NFT = FF // P
NE = 8
FE = 7 * D // 2
FCH = 512
NFC = FE // FCH
ALPHA = (2.0 * DEPTH) ** 0.25
EPS = 1e-5 / ALPHA ** 2
RING = 6
SLOT = 2048
MAGIC = 12582912.0
TWO_PI = (6.28125, 0.0019350051879882812, 2 * math.pi - 6.28125 - 0.0019350051879882812)
PI_SAFE = 3.1415925
NBANK = 8
MAXPASS = 3 * NE
C_BIN, C_LN1G, C_LN1B, C_LN2G, C_LN2B, C_PS, C_BG, C_END = 0, 48, 64, 80, 88, 96, 104, 112


def weight_plan(w):
    plan = []

    def add(key, src, k, n):
        plan.append((key, src.rearrange("(k p) n -> p k n", p=P) if len(src.shape) == 2 else src, k, n))

    for l in range(DEPTH):
        win = w["w_in"][l]
        for key, at in [(("ub", l), PW), (("ua", l), 0)] + [(("gate", l, n), PW + SW + 512 * n) for n in range(4)]:
            for h in range(2):
                add((*key, h), win[512 * h:512 * h + 512, at:at + 512], 4, 512)
        add(("wpool", l), w["w_pool"][l].rearrange("g c d -> c g d"), 4, P)
        for h in range(2):
            add(("pa", l, h), w["w_proj_a"][l][:, 512 * h:512 * h + 512], 4, 512)
        add(("glu", l), w["w_glu"][l], 4, 512)
        for h in range(2):
            add(("pb", l, h), w["w_proj_b"][l][:, 512 * h:512 * h + 512], 4, 512)
        for m in range(4):
            add(("out", l, m), w["w_out"][l][:, 256 * m:256 * m + 256], 8, 256)
        if l == 0:
            for c in range(NFT // 2):
                for name in ("w_ffn_gate", "w_ffn_up"):
                    add((name, c), w[name][0][:, 256 * c:256 * c + 256], 8, 256)
            for m in range(4):
                for a in range(0, NFT, 8):
                    b = min(a + 8, NFT)
                    add(("down", m, a), w["w_ffn_down"][0][P * a:P * b, 256 * m:256 * m + 256], b - a, 256)
    return plan


PASS_SLOTS = []
for _f in range(NFC + 1):
    if _f < NFC:
        PASS_SLOTS += [("gate", _f, 0), ("gate", _f, 1), ("up", _f, 0), ("up", _f, 1)]
    if _f > 0:
        PASS_SLOTS += [("down", _f - 1, 0), ("down", _f - 1, 1)]
PER_PASS = len(PASS_SLOTS)


def psum_plan():
    tiles = [(("prm",), "d")] + [(("x", k), "ad"[k % 2]) for k in range(KD)]

    def s5_matrices(l):
        return ([(("w1t", l, r, i), "a") for r in range(2) for i in range(4)]
                + [(("kern", l, i), "d") for i in range(NG // 4)])

    for l in range(DEPTH):
        tiles += [(("ub", l, h), "d") for h in range(3)] + [(("ua", l, m), "a") for m in range(4)]
        if l == 0:
            tiles += [(("ct", l, r), "d") for r in range(2)]
        tiles += [(("ut", l, i), "a") for i in range(3)] + [(("pd", l), "d")]
        tiles += [(("gate", l, m), "a") for m in range(16)]
        tiles += [(("h0", l, r), "a") for r in range(2)] + [(("rows", l, s), "a") for s in range(2)]
        if l == 0:
            tiles += s5_matrices(l)
        tiles += [(("chunk", l, r), "d") for r in range(3)] + [(("mix", l, g), "a") for g in range(4)]
        tiles += [(("pa", l, m), "d") for m in range(KD)]
        tiles += [(("y", l, i), "ad"[i % 2]) for i in range(NG // 4)]
        tiles += [(("yt", l, k), "a") for k in range(4)] + [(("ytd", l), "a"), (("state", l), "a"), (("stated", l), "a")]
        tiles += [(("glu", l, m), "a") for m in range(4)]
        tiles += [(("pb", l, m), "d") for m in range(KD)] + [(("out", l, m), "d") for m in range(KD)]
        tiles += [(("mean", l, 0), "d"), (("var", l, 0), "d")]
        if l == 0:
            for f in range(NFT):
                tiles += [(("fg", f), "a"), (("fu", f), "d")]
                if f == 3:
                    tiles += [(("ct", 1, r), "d") for r in range(2)]
            tiles += s5_matrices(1)
            tiles += [(("down", m), "d") for m in range(KD)] + [(("mean", l, 1), "d"), (("var", l, 1), "d")]
    tiles += [(("logit",), "d")] + [(("xtok", i), "a") for i in range(6)] + [(("pos",), "d")]
    tiles += [(("gather0", 0), "a"), (("gather0", 1), "d")]
    return tiles


class Tiles:

    def __init__(self, tiles):
        self.keys = [k for k, _ in tiles]
        self.filled = {k: i + 1 for i, (k, _) in enumerate(tiles)}
        count = {"a": 0, "d": 0}
        self.emptied = {}
        for k, owner in tiles:
            count[owner] += 1
            self.emptied[k] = (owner, count[owner])
        self.count = count
        self.bank = {k: i % NBANK for i, k in enumerate(self.keys)}


PASS_TILES = []
for _f in range(NFC + 1):
    if _f < NFC:
        PASS_TILES += [(("g", _f), "a", 2 * (_f % 2)), (("u", _f), "d", 2 * (_f % 2) + 1)]
    if _f == 0:
        PASS_TILES += [(("spread",), "a", 7)]
    if _f == NFC:
        PASS_TILES += [(("gather", 0), "a", 2), (("gather", 1), "d", 3)]
    if _f > 0:
        PASS_TILES += [(("hT", _f - 1), "a", 6 + (_f - 1) % 2)]
PASS_TILES += [(("ye", 0), "a", 4), (("ye", 1), "d", 5)]
PASS_TILES += [(("scatter", _i), "d", 7 - _i % 2) for _i in range(6)]


def trunk_kernel(nc, w, outs):
    y_prompt, y_sample, pool_p, re_p, im_p, pool_s, re_s, im_s = outs
    plan = weight_plan(w)
    n_plan = len(plan)
    slot_of = {key: i for i, (key, _, _, _) in enumerate(plan)}
    tiles = Tiles(psum_plan())
    per_pass = Tiles([(k, owner) for k, owner, _ in PASS_TILES])
    pass_bank = {k: b for k, _, b in PASS_TILES}
    assert PER_PASS % RING == 0

    with ExitStack() as ctx:
        def sb(name, shape, dt=F32):
            return ctx.enter_context(nc.sbuf_tensor(name, shape, dt))

        def sem(name):
            return ctx.enter_context(nc.semaphore(name))

        ring = [sb(f"weights{i}", [P, SLOT]) for i in range(RING)]
        xT = sb("xT", [P, KD, T])
        prod_size = NQ * NPOW * GC
        r_all = sb("r_all", [P, max(KD * T, prod_size)])
        rT = r_all[:, 0:KD * T].rearrange("p (k t) -> p k t", k=KD)
        wide = sb("wide", [P, 25 * T])
        wide_t = wide[:, :].rearrange("p (k t) -> p k t", k=25)
        gates = wide_t[:, 0:16, :]
        mT = wide_t[:, 16:24, :]
        hT = wide_t[:, 0:NFT, :]
        prod = r_all[:, 0:prod_size]
        xstage = wide[:, 0:3 * D].rearrange("p (h n) -> p h n", h=3)
        poolT = wide_t[:, 16:20, :]
        WX = PAD + SEQ
        pext = wide[:, 20 * T:20 * T + 4 * WX].rearrange("p (g t) -> p g t", g=4)
        win_a = r_all[:, 0:4 * WX].rearrange("p (g t) -> p g t", g=4)
        win_b = r_all[:, 4 * WX:7 * WX].rearrange("p (g t) -> p g t", g=3)
        oaT = rT[:, 0:4, :]
        yT = rT[:, 4:8, :]

        WORK = 8 * 1024 + 2 * NQ * NPOW * GC
        ssm = sb("ssm", [P, WORK + 4096 + 2 * NG * UC])

        def part(a, pattern=None, **kw):
            n = 1
            for x in kw.pop("of"):
                n *= x
            v = ssm[:, a:a + n]
            return v.rearrange(pattern, **kw) if pattern else v

        def block3(a, x, y, z=None):
            if z is None:
                return part(a, "p (x y) -> p x y", x=x, of=(x, y))
            return part(a, "p (x y z) -> p x y z", x=x, y=y, of=(x, y, z))

        toep = block3(0, NG, P)
        w1T = [block3(4096 + 2048 * r, NQ, P) for r in range(2)]
        vmat = [block3(8192 + 2304 * r, NQ, NPOW, GC) for r in range(2)]
        w1n = [block3(WORK + 2048 * r, NQ, CHUNK, GC) for r in range(2)]
        kern = block3(WORK, NG, P)
        utok = block3(WORK, NG, CHUNK, GC)
        ytok = block3(WORK, CHUNK, NG, GC)
        ucol = block3(WORK + 4096, NG, UC)
        sprev = [block3(WORK + 4096 + NG * UC + NQ * UC * r, NQ, UC) for r in range(2)]
        turned = [r_all[:, 4 * T + 512 * r:4 * T + 512 * r + 512].rearrange("p (q c) -> p q c", q=NQ) for r in range(2)]
        mixed = [wide[:, 20 * T + 512 * r:20 * T + 512 * r + 512].rearrange("p (q c) -> p q c", q=NQ) for r in range(2)]
        gel = block3(WORK + 4096, 4, T)
        std4 = block3(WORK + 4096, 4, T)
        silu_f = block3(WORK + 4096 + 4 * T, 2, T)
        xtok = block3(0, 3, D)
        acc = block3(3072, 3, D)
        xg = block3(6144, KD, P)
        silu_e = [ssm[:, 7168 + 512 * i:7680 + 512 * i] for i in range(2)]
        hid_e = [ssm[:, 8192 + 512 * i:8704 + 512 * i] for i in range(2)]
        hidT_e = [block3(9216 + 512 * i, 4, P) for i in range(2)]
        y_e = ssm[:, 10240:11264]
        pick = block3(11264, 3, P)
        pickg = block3(11648, 3, P)
        spread = ssm[:, 12032:12032 + T]
        NR = MAXPASS + 1
        pos_of = block3(12800, 3, NR)
        sel_of = block3(12900, 3, NR)
        gate_of = block3(13000, 3, NR)
        lnb = block3(13312, 2, D)
        route = [block3(15400 + 24 * i, 3, NE) for i in range(10)]
        small3 = [ssm[:, 15700 + 4 * i:15703 + 4 * i] for i in range(16)]
        stats = block3(15800, 3, 12)
        mv = block3(15840, 3, 2)

        bnat = sb("bnat", [P, 2, NQ, GC])
        bbar = sb("bbar", [P, 2, NQ, GC])
        cnat = sb("cnat", [P, 2, 4, 2, NS])
        ctr = sb("ctr", [P, 2, NQ, GC])
        h0n = sb("h0n", [P, 2, P])
        spool = sb("spool", [NDEC * PSTATE, PW])
        prm = r_all[0:96, 0:P]
        dtrow = r_all[0:96, P:P + 2]
        cols = r_all[0:C_END, 2 * P:3 * P]
        dsk = r_all[0:DEPTH * NG, 3 * P:3 * P + GC]
        iota_i = r_all[:, 4 * P:5 * P].bitcast(I32)
        prmT = sb("prmT", [P, 96])
        colT = sb("colT", [P, C_END])
        colH = sb("colH", [P, C_END])
        colD = sb("colD", [P, 8])
        dskT = sb("dskT", [GC, DEPTH * NG])
        tiny = sb("tiny", [P, 20, DEPTH * NQ])
        powr = sb("powr", [P, 2, NQ, NPOW])
        powv = sb("powv", [P, 2, NQ, CHUNK])
        turn = sb("turn", [P, 2, NQ, NCH])
        decay = sb("decay", [P, NQ, NCH])
        scr = sb("scr", [P, 2, NQ * NCH // 2])
        ident = sb("ident", [P, P])
        tri = sb("tri", [P, P])
        ones = sb("ones", [P, P])
        avg = sb("avg", [P, P])
        iota = sb("iota", [P, P])
        pmask = sb("pmask", [NDEC * PSTATE, 4, NDEC])
        rcount = sb("rcount", [P, 4, PAD])
        ubias = sb("ubias", [P, SW])
        udec = sb("udec", [P, 4, NDEC])
        pdec = sb("pdec", [P, 4, NDEC])
        pfix = sb("pfix", [P, PAD])
        rows = [spool[0:PSTATE, :], sb("rows_d", [NDEC, PW])[:, :]]
        srow = sb("srow", [P, 2, P])
        srow_p = sb("srow_p", [NQ, 2, P])
        sfin = sb("sfin", [P, 2, NQ])
        sfin_d = sb("sfin_d", [P, 2, NDEC, NQ])
        consts = sb("consts", [P, 4])
        npass_i = sb("npass_i", [1, 1], I32)
        wrt = sb("wrt", [P, KD, NE])
        brt = sb("brt", [P, NE])
        bank = [ctx.enter_context(nc.psum_tensor(f"bank{i}", [P, 512], F32)) for i in range(NBANK)]

        landed = [sem(f"weights_landed{i}") for i in range(RING)]
        used = sem("weights_used")
        filled = sem("tiles_filled")
        emptied = {"a": sem("tiles_emptied_by_act"), "d": sem("tiles_emptied_by_dve")}
        x_in, prm_in, layer_in, router_in, lnb_in, stored = map(
            sem, ("x_in", "params_in", "layer_in", "router_in", "lnb_in", "stored"))
        pool_step, dve_step = sem("gpsimd_step"), sem("dve_step")
        const_ready, prm_rows, prm_ready = sem("constants_ready"), sem("prm_rows_ready"), sem("params_transposed")
        exp_arg, exp_ready, trig_arg, trig_ready = map(sem, ("exp_arg", "exp_ready", "trig_arg", "trig_ready"))
        vmat_ready, bbar_ready, w1n_ready = sem("vmat_ready"), sem("bbar_ready"), sem("w1n_ready")
        kern_ready, toep_zero, toep_ready, utok_zero = map(sem, ("kern_ready", "toep_zero", "toep_ready", "utok_zero"))
        pext_zero, udec_ready, pool_ready = sem("pext_zero"), sem("udec_ready"), sem("pool_ready")
        sprev_ready, sfin_ready = sem("sprev_ready"), sem("sfin_ready")
        gelu_arg, gelu_tanh, y_ready, ob_ready, m_ready = map(
            sem, ("gelu_arg", "gelu_tanh", "y_ready", "ob_ready", "merged_ready"))
        centred, squared, std_ready, norm_ready, x_next = map(
            sem, ("centred", "squared", "std_ready", "norm_ready", "x_next"))
        rows_out, states_out = sem("rows_out"), sem("states_out")
        sel_ready, rexp_arg, rexp_ready, npass_ready = map(
            sem, ("sel_ready", "router_exp_arg", "router_exp_ready", "npass_ready"))
        pick_ready, pickg_ready = sem("pick_ready"), sem("pickg_ready")
        fvar_ready, fstd_ready, y_out = sem("final_var"), sem("final_std"), sem("final_y")

        def tile_in(eng, key):
            eng.wait_ge(filled, tiles.filled[key])
            return bank[tiles.bank[key]]

        def wait_emptied(eng, key):
            owner, n = tiles.emptied[key]
            eng.wait_ge(emptied[owner], n)

        def pass_tile_in(eng, key, i):
            eng.wait_ge(filled, i * len(per_pass.keys) + (len(tiles.keys) + per_pass.filled[key]))
            return bank[pass_bank[key]]

        def wait_pass_emptied(eng, key, i, back=0):
            owner, n = per_pass.emptied[key]
            eng.wait_ge(emptied[owner],
                        i * per_pass.count[owner] + (tiles.count[owner] + n - back * per_pass.count[owner]))

        LAYER_DMAS = 10

        def all_passes(eng):
            eng.wait_ge(npass_ready, 1)
            return eng.Fori(0, eng.value_load(npass_i[0:1, 0:1], min_val=NE, max_val=MAXPASS))

        block = ctx.enter_context(nc.Block())

        @block.sync
        def _(sp):
            for jj in range(CHUNK):
                h, at = jj // 4, 32 * (jj % 4)
                sp.dma_start(xstage[at:at + 32, h, :],
                             w["x_prompt"][0].rearrange("(c j) n -> j c n", j=CHUNK)[jj]).then_inc(x_in, 16)
            sp.dma_start(xstage[0:NDEC, 2, :], w["x_sample"].rearrange("b o n -> (b o) n")).then_inc(x_in, 16)
            for i, (key, src, k, n) in enumerate(plan):
                if i >= RING:
                    sp.wait_ge(used, i - RING + 1)
                sp.dma_start(ring[i % RING][:, 0:k * n].rearrange("p (k n) -> p k n", k=k), src)\
                    .then_inc(landed[i % RING], 16)

            def expert_weights(e, ahead):
                for s, (what, f, h) in enumerate(PASS_SLOTS):
                    i = (n_plan + s) % RING
                    sp.wait_ge(used, ahead + (s - RING + 1))
                    if what == "down":
                        src = w["w_moe_down"][0][bass.ds(e, 1), FCH * f + 256 * h:FCH * f + 256 * h + 256, :]
                    else:
                        src = w["w_moe_" + what][0][bass.ds(e, 1), 512 * h:512 * h + 512, FCH * f:FCH * f + FCH]
                    k = src.shape[1] // P
                    sp.dma_start(ring[i][:, :].rearrange("p (k n) -> p k n", k=k),
                                 src.rearrange("a (k p) n -> p (a k) n", p=P)).then_inc(landed[i], 16)

            with sp.Fori(0, NE) as e:
                expert_weights(e, e * PER_PASS + n_plan)
            sp.wait_ge(npass_ready, 1)
            npass = sp.value_load(npass_i[0:1, 0:1], min_val=NE, max_val=MAXPASS)
            for c in (1, 2):
                with sp.If(npass > c * NE):
                    with sp.Fori(0, NE) as e:
                        expert_weights(e, e * PER_PASS + (n_plan + c * NE * PER_PASS))

        @block.gpsimd
        def _(pool):
            n_step = 0

            def step(ins):
                nonlocal n_step
                n_step += 1
                ins.then_inc(pool_step, 1)
                pool.wait_ge(pool_step, n_step)

            def ready(ins):
                nonlocal n_const
                n_const += 1
                ins.then_inc(const_ready, 1)
                pool.wait_ge(const_ready, n_const)

            n_const = 0
            step(pool.memset(ident[:, :], 0.0))
            ready(pool.affine_select(out=ident[:, :], in_=ident[:, :], compare_op=ALU.not_equal, fill=1.0, base=0,
                                     pattern=[[-1, P]], channel_multiplier=1))
            step(pool.iota(iota_i[:, :], pattern=[[1, P]], base=0, channel_multiplier=0))
            ready(pool.tensor_copy(iota[:, :], iota_i[:, :]))
            ready(pool.memset(avg[:, :], 1.0 / D))
            ready(pool.memset(consts[:, 0:1], EPS))
            ready(pool.memset(consts[:, 1:2], math.pi / 2))
            pool.memset(utok[NCH:UC, :, :, :], 0.0).then_inc(utok_zero, 1)
            pool.wait_ge(utok_zero, 1)
            step(pool.memset(pmask[:, :, :], 1.0))
            step(pool.affine_select(out=pmask[:, :, :], in_=pmask[:, :, :], compare_op=ALU.is_ge, fill=0.0,
                                    base=PSTATE - 1, pattern=[[0, 4], [PSTATE, NDEC]], channel_multiplier=-1))
            for g, wd in enumerate(WINDOWS):
                ready(pool.affine_select(out=pmask[:, g, :], in_=pmask[:, g, :], compare_op=ALU.is_ge, fill=0.0,
                                         base=-(PSTATE + 1 - wd), pattern=[[-PSTATE, NDEC]], channel_multiplier=1))
            pool.memset(toep[:, :, :], 0.0).then_inc(toep_zero, 1)
            pool.wait_ge(toep_zero, 1)
            ready(pool.memset(ones[:, :], 1.0))
            step(pool.memset(tri[:, :], 1.0))
            ready(pool.affine_select(out=tri[:, :], in_=tri[:, :], compare_op=ALU.is_gt, fill=0.0, base=0,
                                     pattern=[[1, P]], channel_multiplier=-1))

            def toeplitz(l):
                pool.wait_ge(kern_ready, l + 1)
                if l == 0:
                    pool.wait_ge(toep_zero, 1)
                for j in range(CHUNK):
                    pool.dma_start(toep[GC * j:GC * j + GC, :, GC * j:P], kern[0:GC, :, 0:P - GC * j])\
                        .then_inc(toep_ready, 16)

            n_stored = 0
            for l in range(DEPTH):
                pool.dma_start(pool_s[l, :, 0:PSTATE - 1, :].rearrange("b r n -> b (r n)"),
                               w["state_pool"][l, :, 1:PSTATE, :].rearrange("b r n -> b (r n)")).then_inc(stored, 16)
                if l == 1:
                    toeplitz(l)
                    pool.wait_ge(toep_ready, 16 * CHUNK * 2)
                    pool.memset(utok[NCH:UC, :, :, :], 0.0).then_inc(utok_zero, 1)
                wait_emptied(pool, ("rows", l, 1))
                pool.dma_start(pool_p[l, 0], rows[0]).then_inc(rows_out, 16)
                pool.dma_start(pool_s[l, :, PSTATE - 1, :], rows[1]).then_inc(rows_out, 16)
                if l == 0:
                    toeplitz(l)
                wait_emptied(pool, ("stated", l))
                for r, (one, dec) in enumerate(((re_p, re_s), (im_p, im_s))):
                    pool.dma_start(one[l].rearrange("a g p -> (a g p)").rearrange("(q n) -> q n", n=P),
                                   srow_p[:, r, :]).then_inc(states_out, 16)
                    pool.dma_start(dec[l].rearrange("b g p -> (b g p)").rearrange("(q n) -> q n", n=P),
                                   srow[:, r, :]).then_inc(states_out, 16)
                n_stored += 1
            pool.wait_ge(x_next, 3 * KD)
            for i, name in enumerate(("ln2_g", "ln2_b")):
                pool.dma_start(lnb[:, i, :], w[name][DEPTH - 1].partition_broadcast(P)).then_inc(lnb_in, 16)
            for h, (_, m) in enumerate(TILES):
                pool.wait_ge(y_out, h + 1)
                if m == P:
                    for jl in range(4):
                        pool.dma_start(y_prompt[0].rearrange("(c j) n -> j c n", j=CHUNK)[4 * h + jl],
                                       acc[32 * jl:32 * jl + 32, h, :]).then_inc(stored, 16)
                        n_stored += 1
                else:
                    pool.dma_start(y_sample.rearrange("b o n -> (b o) n"), acc[0:m, h, :]).then_inc(stored, 16)
                    n_stored += 1
            pool.wait_ge(rows_out, 16 * 2 * DEPTH)
            pool.wait_ge(states_out, 16 * 4 * DEPTH)
            pool.wait_ge(stored, 16 * n_stored)

        @block.scalar
        def _(act):
            def load_layer(l):
                for r, (b, c, s) in enumerate((("b_re", "c_re", "state_ssm_re"), ("b_im", "c_im", "state_ssm_im"))):
                    act.dma_start(bnat[:, r, :, :], w[b][l].rearrange("(q h) p c -> (h p) q c", h=2)).then_inc(layer_in, 16)
                    for h in range(2):
                        act.dma_start(cnat[:, r, :, h, :], w[c][l].rearrange("(k g) c p -> (g c) k p", k=4))\
                            .then_inc(layer_in, 16)
                    act.dma_start(h0n[:, r, :], w[s][l].rearrange("b g p -> (b g p)").rearrange("(q n) -> q n", n=P))\
                        .then_inc(layer_in, 16)
                act.dma_start(spool[:, :], w["state_pool"][l].rearrange("b r n -> (b r) n")).then_inc(layer_in, 16)
                act.dma_start(ubias[:, :], w["b_in"][l, PW:PW + SW].partition_broadcast(P)).then_inc(layer_in, 16)

            act.dma_start(prm[0:32, :], w["lambda_re"].rearrange("l (q h) p -> (l q) (h p)", h=2)).then_inc(prm_in, 16)
            act.dma_start(prm[32:64, :], w["lambda_im"].rearrange("l (q h) p -> (l q) (h p)", h=2)).then_inc(prm_in, 16)
            act.dma_start(dtrow[64:96, :], w["log_dt"].rearrange("l (q h) -> (l q) h", h=2)).then_inc(prm_in, 16)
            for at, name, n in ((C_BIN, "b_in", 48), (C_LN1G, "ln1_g", 16), (C_LN1B, "ln1_b", 16), (C_LN2G, "ln2_g", 8),
                                (C_LN2B, "ln2_b", 8), (C_PS, "pool_scale", 8), (C_BG, "b_glu", 8)):
                src = w[name].rearrange("l n -> (l n)").rearrange("(r n) -> r n", n=P)[0:n, :]
                act.dma_start(cols[at:at + n, :], src).then_inc(prm_in, 16)
            act.dma_start(dsk[:, :], w["d_skip"].rearrange("l g c -> (l g) c")).then_inc(prm_in, 16)
            load_layer(0)
            act.dma_start(wrt[:, :, :], w["w_router"][0].rearrange("(k p) e -> p k e", p=P)).then_inc(router_in, 16)
            act.dma_start(brt[:, :], w["b_router"][0].partition_broadcast(P)).then_inc(router_in, 16)

            act.wait_ge(prm_ready, 1)
            act.activation(tiny[:, 0, :], prmT[:, 64:96], ACT.Exp).then_inc(exp_ready, 1)
            act.wait_ge(exp_arg, 1)
            act.activation(tiny[:, 2, :], tiny[:, 1, :], ACT.Exp).then_inc(exp_ready, 1)
            act.wait_ge(trig_arg, 1)
            act.wait_ge(const_ready, 5)
            act.activation(tiny[:, 6, :], tiny[:, 4, :], ACT.Sin).then_inc(trig_ready, 1)
            act.activation(tiny[:, 7, :], tiny[:, 5, :], ACT.Sin, bias=consts[:, 1:2], scale=-1.0).then_inc(trig_ready, 1)

            for k in range(0, KD, 2):
                act.activation(xT[:, k, :], tile_in(act, ("x", k))[:, 0:T], ACT.Copy).then_inc(emptied["a"], 1)

            def transposed_w1(l):
                for r in range(2):
                    for i in range(4):
                        act.activation(w1T[r][:, 4 * i:4 * i + 4, :],
                                       tile_in(act, ("w1t", l, r, i))[:, :].rearrange("p (q n) -> p q n", q=4),
                                       ACT.Copy).then_inc(emptied["a"], 1)

            def mixer(l):
                act.wait_ge(prm_ready, 3)
                for m in range(4):
                    ps = tile_in(act, ("ua", l, m))
                    bias = colT[:, C_BIN + 24 * l + m:C_BIN + 24 * l + m + 1]
                    act.activation(udec[:, m, :], ps[:, SEQ:T], ACT.Identity, bias=bias).then_inc(udec_ready, 1)
                    act.activation(pext[:, m, PAD:WX].rearrange("p (c j) -> p j c", j=CHUNK),
                                   ps[:, 0:SEQ].rearrange("p (j c) -> p j c", j=CHUNK), ACT.Identity, bias=bias)\
                        .then_inc(emptied["a"], 1)
                for i in range(3):
                    a, b = 12 * i, min(12 * i + 12, NG)
                    act.activation(ucol[:, a:b, :],
                                   tile_in(act, ("ut", l, i))[:, 0:(b - a) * UC].rearrange("p (g c) -> p g c", c=UC),
                                   ACT.Copy).then_inc(emptied["a"], 1)
                for m in range(16):
                    act.activation(gates[:, m, :], tile_in(act, ("gate", l, m))[:, 0:T], ACT.Tanh, scale=0.5,
                                   bias=colH[:, C_BIN + 24 * l + 8 + m:C_BIN + 24 * l + 9 + m]).then_inc(emptied["a"], 1)
                for r in range(2):
                    act.activation(sprev[r][:, :, NCH:UC],
                                   tile_in(act, ("h0", l, r))[:, 0:P].rearrange("p (b q) -> p q b", q=NQ),
                                   ACT.Copy).then_inc(emptied["a"], 1)
                for s in range(2):
                    n = (PSTATE, NDEC)[s]
                    act.activation(rows[s], tile_in(act, ("rows", l, s))[0:n, :], ACT.Copy).then_inc(emptied["a"], 1)
                if l == 0:
                    transposed_w1(l)
                for g in range(4):
                    act.activation(oaT[:, g, :], tile_in(act, ("mix", l, g))[:, 0:T], ACT.Copy,
                                   scale=colD[:, 4 * l + g:4 * l + g + 1]).then_inc(emptied["a"], 1)
                for i in range(0, NG // 4, 2):
                    to = ytok.rearrange("p j (q h) c -> p h j q c", h=2)[0:UC, 0, :, 2 * i:2 * i + 4, :]
                    act.activation(to,
                                   tile_in(act, ("y", l, i))[0:UC, :].rearrange("p (g j c) -> p j g c", g=4, j=CHUNK),
                                   ACT.Copy).then_inc(emptied["a"], 1)
                for k in range(4):
                    ps = tile_in(act, ("yt", l, k))
                    act.activation(yT[:, k, 0:SEQ], ps[:, 0:SEQ], ACT.Copy, scale=0.5)
                    act.activation(gel[:, k, 0:SEQ], ps[:, 0:SEQ], ACT.Square).then_inc(emptied["a"], 1)
                ps = tile_in(act, ("ytd", l))[:, 0:4 * NDEC].rearrange("p (k b) -> p k b", k=4)
                act.activation(yT[:, :, SEQ:T], ps, ACT.Copy, scale=0.5)
                act.activation(gel[:, :, SEQ:T], ps, ACT.Square).then_inc(emptied["a"], 1)
                if l == 1:
                    act.wait_ge(states_out, 16 * 4)
                act.activation(srow_p[:, :, :], tile_in(act, ("state", l))[0:NQ, 0:2 * P]
                               .rearrange("p (r n) -> p r n", r=2), ACT.Copy).then_inc(emptied["a"], 1)
                act.activation(srow[:, :, :], tile_in(act, ("stated", l))[:, 0:2 * P]
                               .rearrange("p (r n) -> p r n", r=2), ACT.Copy).then_inc(emptied["a"], 1)
                for k in range(4):
                    act.wait_ge(gelu_arg, 4 * l + k + 1)
                    act.activation(gel[:, k, :], gel[:, k, :], ACT.Tanh, scale=2.0 * math.sqrt(2.0 / math.pi))\
                        .then_inc(gelu_tanh, 1)
                act.wait_ge(y_ready, 4 * l + 4)
                for m in range(4):
                    act.activation(gel[:, m, :], tile_in(act, ("glu", l, m))[:, 0:T], ACT.Tanh, scale=0.5,
                                   bias=colH[:, C_BG + 4 * l + m:C_BG + 4 * l + m + 1]).then_inc(emptied["a"], 1)

            def layer_norm(l, which):
                n = 2 * l + which
                for h in range(2):
                    if h == 0:
                        act.wait_ge(centred, n + 1)
                    else:
                        wait_emptied(act, ("mean", l, which))
                    act.activation(mT[:, 4 * h:4 * h + 4, :], rT[:, 4 * h:4 * h + 4, :], ACT.Square).then_inc(squared, 1)
                act.activation(std4[:, 0, :], tile_in(act, ("var", l, which))[:, 0:T], ACT.Sqrt, bias=consts[:, 0:1])\
                    .then_inc(std_ready, 1)
                at = (C_LN1B + KD * l) if which == 0 else C_LN2B
                for k in range(KD):
                    act.wait_ge(norm_ready, KD * n + k + 1)
                    act.activation(xT[:, k, :], rT[:, k, :], ACT.Identity, bias=colT[:, at + k:at + k + 1])\
                        .then_inc(x_next, 1)

            def dense_ffn():
                act.wait_ge(rows_out, 16 * 2)
                load_layer(1)
                for f in range(NFT):
                    if f >= 2:
                        wait_emptied(act, ("fu", f - 2))
                    act.activation(silu_f[:, f % 2, :], tile_in(act, ("fg", f))[:, 0:T], ACT.Silu)\
                        .then_inc(emptied["a"], 1)
                transposed_w1(1)

            mixer(0)
            layer_norm(0, 0)
            dense_ffn()
            layer_norm(0, 1)
            mixer(1)
            layer_norm(1, 0)

            for i in range(6):
                h, half = i // 2, i % 2
                m = TILES[h][1]
                act.activation(xtok[0:m, h, 512 * half:512 * half + 512], tile_in(act, ("xtok", i))[0:m, :], ACT.Copy)\
                    .then_inc(emptied["a"], 1)
            act.wait_ge(rexp_arg, 1)
            act.activation(small3[3], small3[2], ACT.Exp).then_inc(rexp_ready, 1)
            act.activation(xg[:, 0:4, :], tile_in(act, ("gather0", 0))[:, :].rearrange("p (k s) -> p k s", k=4), ACT.Copy)\
                .then_inc(emptied["a"], 1)

            def one_pass(i):
                def copy_hidden(f):
                    g = (f - 2) % NFC
                    act.wait_ge(used, i * PER_PASS + (n_plan + PASS_SLOTS.index(("down", g, 1)) + 1
                                                      - (PER_PASS if f < 2 else 0)))
                    act.activation(hidT_e[f % 2], pass_tile_in(act, ("hT", f), i)[:, :]
                                   .rearrange("p (f s) -> p f s", f=4), ACT.Copy).then_inc(emptied["a"], 1)

                for f in range(NFC):
                    wait_pass_emptied(act, ("u", (f - 2) % NFC), i, back=int(f < 2))
                    act.activation(silu_e[f % 2], pass_tile_in(act, ("g", f), i)[:, :], ACT.Silu)\
                        .then_inc(emptied["a"], 1)
                    if f == 0:
                        act.activation(spread, pass_tile_in(act, ("spread",), i)[:, 0:T], ACT.Copy)\
                            .then_inc(emptied["a"], 1)
                    else:
                        copy_hidden(f - 1)
                act.activation(xg[:, 0:4, :], pass_tile_in(act, ("gather", 0), i)[:, :]
                               .rearrange("p (k s) -> p k s", k=4), ACT.Copy).then_inc(emptied["a"], 1)
                copy_hidden(NFC - 1)
                act.activation(y_e[:, 0:512], pass_tile_in(act, ("ye", 0), i)[:, :], ACT.Copy, scale=1.0 / ALPHA)\
                    .then_inc(emptied["a"], 1)

            with all_passes(act) as i:
                one_pass(i)
            act.wait_ge(fvar_ready, 1)
            act.activation(small3[11], small3[10], ACT.Sqrt).then_inc(fstd_ready, 1)

        @block.vector
        def _(dve):
            n_step = 0

            def step(ins):
                nonlocal n_step
                n_step += 1
                ins.then_inc(dve_step, 1)
                dve.wait_ge(dve_step, n_step)

            def tt(out, a, b, op):
                return dve.tensor_tensor(out, a, b, op)

            def complex_mul(out, a, b, t):
                tt(t[0], a[0], b[0], ALU.mult)
                step(tt(t[1], a[1], b[1], ALU.mult))
                step(tt(out[0], t[0], t[1], ALU.subtract))
                tt(t[0], a[0], b[1], ALU.mult)
                step(tt(t[1], a[1], b[0], ALU.mult))
                step(tt(out[1], t[0], t[1], ALU.add))

            (DT, ARE, MOD, AIM, RED, ABS, SIN, COS, LBR, LBI, FR, FI, UR, UI, MOD8, T0, T1, T2) = (
                tiny[:, i, :] for i in range(18))
            lre, lim = prmT[:, 0:32], prmT[:, 32:64]

            dve.wait_ge(prm_in, 16 * 11)
            dve.tensor_copy(prm[64:96, :].rearrange("p (h n) -> p h n", h=2),
                            dtrow[64:96, :].unsqueeze(2).to_broadcast([32, 2, NS])).then_inc(prm_rows, 1)
            ps = tile_in(dve, ("prm",))
            dve.tensor_copy(prmT[:, :], ps[:, 0:96]).then_inc(prm_ready, 1)
            dve.tensor_copy(dskT[:, :], ps[0:GC, 208:272]).then_inc(prm_ready, 1)
            step(dve.tensor_copy(colT[:, :], ps[:, 96:208]))
            dve.tensor_scalar(colH[:, :], colT[:, :], 0.5, None, ALU.mult).then_inc(prm_ready, 1)
            dve.tensor_scalar(colD[:, :], colT[:, C_PS:C_PS + 8], 2.0, None, ALU.mult).then_inc(emptied["d"], 1)

            for k in range(1, KD, 2):
                dve.tensor_copy(xT[:, k, :], tile_in(dve, ("x", k))[:, 0:T]).then_inc(emptied["d"], 1)

            def angles():
                dve.wait_ge(exp_ready, 1)
                tt(ARE, lre, DT, ALU.mult).then_inc(exp_arg, 1)
                step(tt(AIM, lim, DT, ALU.mult))
                step(dve.tensor_scalar(T0, AIM, 1.0 / (2.0 * math.pi), MAGIC, ALU.mult, ALU.add))
                step(dve.tensor_scalar(T0, T0, MAGIC, None, ALU.subtract))
                last = AIM
                for c in TWO_PI:
                    step(dve.scalar_tensor_tensor(out=RED, in0=T0, scalar=-c, in1=last, op0=ALU.mult, op1=ALU.add))
                    last = RED
                step(dve.tensor_scalar(RED, RED, PI_SAFE, -PI_SAFE, ALU.min, ALU.max))
                step(dve.tensor_scalar(T1, RED, -1.0, None, ALU.mult))
                tt(ABS, RED, T1, ALU.max).then_inc(trig_arg, 1)
                dve.wait_ge(exp_ready, 2)
                step(tt(T0, MOD, MOD, ALU.mult))
                step(tt(T0, T0, T0, ALU.mult))
                step(tt(MOD8, T0, T0, ALU.mult))
                dve.wait_ge(trig_ready, 2)
                complex_mul((UR, UI), (COS, SIN), (COS, SIN), (T0, T1))
                complex_mul((LBR, LBI), (UR, UI), (UR, UI), (T0, T1))
                complex_mul((UR, UI), (LBR, LBI), (LBR, LBI), (T0, T1))
                tt(LBR, MOD, COS, ALU.mult)
                tt(LBI, MOD, SIN, ALU.mult)
                tt(T0, lre, lre, ALU.mult)
                step(tt(T1, lim, lim, ALU.mult))
                step(tt(T0, T0, T1, ALU.add))
                step(dve.reciprocal(T0, T0))
                step(dve.tensor_scalar(T1, LBR, 1.0, None, ALU.subtract))
                tt(FR, T1, lre, ALU.mult)
                step(tt(T2, LBI, lim, ALU.mult))
                step(tt(FR, FR, T2, ALU.add))
                tt(FR, FR, T0, ALU.mult)
                tt(FI, LBI, lre, ALU.mult)
                step(tt(T2, T1, lim, ALU.mult))
                step(tt(FI, FI, T2, ALU.subtract))
                step(tt(FI, FI, T0, ALU.mult))

            def s5_tables(l):
                L = slice(NQ * l, NQ * l + NQ)

                def pair(tab, a, b):
                    return tab[:, 0, :, a:b], tab[:, 1, :, a:b]

                def wide_pair(p, n):
                    return tuple(x.to_broadcast([P, NQ, n]) for x in p)

                def work_pair(n):
                    return tuple(scr[:, r, 0:NQ * n].rearrange("p (q n) -> p q n", q=NQ) for r in range(2))

                for tab, first in ((powr, (LBR, LBI)), (turn, (UR, UI))):
                    dve.memset(tab[:, 0, :, 0:1], 1.0)
                    dve.memset(tab[:, 1, :, 0:1], 0.0)
                    dve.tensor_copy(tab[:, 0, :, 1:2], first[0][:, L].unsqueeze(2))
                    step(dve.tensor_copy(tab[:, 1, :, 1:2], first[1][:, L].unsqueeze(2)))
                n = 2
                while n < NPOW:
                    h = n // 2
                    complex_mul(pair(powr, h + 1, n + 1), pair(powr, 1, h + 1), wide_pair(pair(powr, h, h + 1), h),
                                work_pair(h))
                    n *= 2
                for j in range(CHUNK):
                    dve.tensor_copy(powv[:, :, :, j], powr[:, :, :, CHUNK - 1 - j])
                n = 2
                while n < NCH:
                    complex_mul(pair(turn, n, n + 1), pair(turn, n // 2, n // 2 + 1), pair(turn, n // 2, n // 2 + 1),
                                work_pair(1))
                    complex_mul(pair(turn, n + 1, 2 * n), pair(turn, 1, n), wide_pair(pair(turn, n, n + 1), n - 1),
                                work_pair(n - 1))
                    n *= 2
                dve.memset(decay[:, :, 0:1], 0.0)
                dve.tensor_copy(decay[:, :, 1:NCH], MOD8[:, L].unsqueeze(2).to_broadcast([P, NQ, NCH - 1]))
                dve.wait_ge(layer_in, 16 * LAYER_DMAS * (l + 1))
                complex_mul((bbar[:, 0, :, :], bbar[:, 1, :, :]),
                            tuple(x[:, L].unsqueeze(2).to_broadcast([P, NQ, GC]) for x in (FR, FI)),
                            (bnat[:, 0, :, :], bnat[:, 1, :, :]), work_pair(GC))

            def c_rows(l):
                for r in range(2):
                    ps = tile_in(dve, ("ct", l, r))[:, :].rearrange("p (q h c) -> p q h c", h=2, c=GC)
                    dve.tensor_copy(ctr[0:NS, r, :, :], ps[0:NS, :, 0, :])
                    dve.tensor_copy(ctr[NS:P, r, :, :], ps[NS:P, :, 1, :]).then_inc(emptied["d"], 1)

            def product(out, minus, powers, mat, n):
                pw = [powers[:, r, :, :].unsqueeze(3).to_broadcast([P, NQ, n, GC]) for r in range(2)]
                mt = [mat[:, r, :, :].unsqueeze(2).to_broadcast([P, NQ, n, GC]) for r in range(2)]
                t4 = prod[:, 0:NQ * n * GC].rearrange("p (q n c) -> p q n c", q=NQ, n=n)
                tt(out[0], pw[0], mt[0], ALU.mult)
                step(tt(t4, pw[1], mt[1], ALU.mult))
                step(tt(out[0], out[0], t4, ALU.subtract))
                tt(out[1], pw[0], mt[1], ALU.mult)
                step(tt(t4, pw[1], mt[0], ALU.mult))
                if not minus:
                    return tt(out[1], out[1], t4, ALU.add)
                flat = [x.rearrange("p q n c -> p (q n c)") for x in (out[1], t4)]
                return dve.scalar_tensor_tensor(out=flat[0], in0=flat[0], scalar=-1.0, in1=flat[1],
                                                op0=ALU.mult, op1=ALU.subtract)

            def s5_outputs(l):
                c_wait = tiles.emptied[("ct", l, 1)][1]
                dve.wait_ge(emptied["d"], c_wait)
                product(vmat, True, powr, ctr, NPOW).then_inc(vmat_ready, 1)
                dve.wait_ge(vmat_ready, l + 1)

            def s5_inputs(l):
                product(w1n, False, powv, bbar, CHUNK).then_inc(w1n_ready, 1)
                dve.wait_ge(w1n_ready, l + 1)

            def kernel_rows(l):
                for i in range(NG // 4):
                    to = kern.rearrange("p (q h) n -> p h q n", h=2)[0:GC, i % 2, 4 * (i // 2):4 * (i // 2) + 4, :]
                    dve.tensor_copy(to,
                                    tile_in(dve, ("kern", l, i))[0:GC, :].rearrange("p (g n) -> p g n", g=4))\
                        .then_inc(emptied["d"], 1)
                skip = scr[0:GC, :, :].rearrange("p r n -> p (r n)").rearrange("p (g c) -> p g c", g=NG)
                step(tt(skip, ident[0:GC, 0:GC].unsqueeze(1).to_broadcast([GC, NG, GC]),
                        dskT[:, NG * l:NG * l + NG].unsqueeze(2).to_broadcast([GC, NG, GC]), ALU.mult))
                wait_emptied(dve, ("kern", l, NG // 4 - 1))
                tt(kern[0:GC, :, 0:GC], kern[0:GC, :, 0:GC], skip, ALU.add).then_inc(kern_ready, 1)

            def s5_columns(l):
                dve.wait_ge(layer_in, 16 * LAYER_DMAS * (l + 1))
                if l == 1:
                    dve.wait_ge(toep_ready, 16 * CHUNK * 2)
                for h in range(2):
                    ps = tile_in(dve, ("ub", l, h))
                    for jl in range(4):
                        q = slice(32 * jl, 32 * jl + 32)
                        ins = tt(utok[0:NCH, :, 4 * h + jl, :], ps[q, :].rearrange("p (g c) -> p g c", g=NG),
                                 ubias[q, :].rearrange("p (g c) -> p g c", g=NG), ALU.add)
                    ins.then_inc(emptied["d"], 1)
                ps = tile_in(dve, ("ub", l, 2))
                dve.wait_ge(utok_zero, l + 1)
                for j in (0, CHUNK - 1):
                    ins = tt(utok[NCH:UC, :, j, :], ps[0:NDEC, :].rearrange("p (g c) -> p g c", g=NG),
                             ubias[0:NDEC, :].rearrange("p (g c) -> p g c", g=NG), ALU.add)
                ins.then_inc(emptied["d"], 1)

            def pooling(l):
                step(dve.memset(pext[:, :, 0:PAD], 0.0))
                if l == 0:
                    dve.wait_ge(const_ready, 9)
                    for g, wd in enumerate(WINDOWS):
                        ins = dve.tensor_scalar(rcount[:, g, :], iota[:, 0:PAD], 1.0, float(wd), ALU.add, ALU.min)
                    step(ins)
                    step(dve.reciprocal(rcount[:, :, :], rcount[:, :, :]))
                wait_emptied(dve, ("ua", l, 3))
                step(tt(win_a[:, :, 1:WX], pext[:, :, 1:WX], pext[:, :, 0:WX - 1], ALU.add))
                step(tt(win_b[:, :, 3:WX], win_a[:, 1:4, 3:WX], win_a[:, 1:4, 1:WX - 2], ALU.add))
                step(tt(win_a[:, 2:4, 7:WX], win_b[:, 1:3, 7:WX], win_b[:, 1:3, 3:WX - 4], ALU.add))
                step(tt(win_b[:, 2, PSTATE:WX], win_a[:, 3, PSTATE:WX], win_a[:, 3, 7:WX - 8], ALU.add))
                sums = (win_a[:, 0, :], win_b[:, 0, :], win_a[:, 2, :], win_b[:, 2, :])
                step(tt(pdec[:, :, :], tile_in(dve, ("pd", l))[:, 0:4 * NDEC].rearrange("p (g b) -> p g b", g=4),
                        udec[:, :, :], ALU.add))
                for g, wd in enumerate(WINDOWS):
                    def steps(v, n):
                        return v.rearrange("p (c j) -> p c j", j=CHUNK)[:, 0:n, :]

                    out = poolT[:, g, 0:SEQ].rearrange("p (j c) -> p c j", j=CHUNK)
                    step(dve.scalar_tensor_tensor(out=out, in0=steps(sums[g][:, PAD:WX], NCH), scalar=1.0 / wd,
                                                  in1=steps(pext[:, g, PAD:WX], NCH), op0=ALU.mult, op1=ALU.subtract))
                    step(tt(pfix[:, :], sums[g][:, PAD:2 * PAD], rcount[:, g, :], ALU.mult))
                    tt(out[:, 0:2, :], steps(pfix[:, :], 2), steps(pext[:, g, PAD:2 * PAD], 2), ALU.subtract)
                    ins = dve.scalar_tensor_tensor(out=poolT[:, g, SEQ:T], in0=pdec[:, g, :], scalar=1.0 / wd,
                                                   in1=udec[:, g, :], op0=ALU.mult, op1=ALU.subtract)
                    if g < 3:
                        step(ins)
                    else:
                        ins.then_inc(emptied["d"], 1)

            def states(l):
                L = slice(NQ * l, NQ * l + NQ)
                er, ei = turn[:, 0, :, :], turn[:, 1, :, :]
                ar, ai, dec = (tile_in(dve, ("chunk", l, r)) for r in range(3))
                ar, ai = (x[:, :].rearrange("p (q c) -> p q c", q=NQ) for x in (ar, ai))
                tt(turned[0], er, ar, ALU.mult)
                tt(mixed[1], ei, ar, ALU.mult).then_inc(emptied["d"], 1)
                tt(turned[1], er, ai, ALU.mult)
                tt(mixed[0], ei, ai, ALU.mult).then_inc(emptied["d"], 1)
                wait_emptied(dve, ("chunk", l, 1))
                tt(turned[0], turned[0], mixed[0], ALU.add)
                step(tt(turned[1], turned[1], mixed[1], ALU.subtract))
                for r in range(2):
                    ins = dve.tensor_tensor_scan(mixed[r].rearrange("p q c -> p (q c)"),
                                                 decay[:, :, :].rearrange("p q c -> p (q c)"),
                                                 turned[r].rearrange("p q c -> p (q c)"), 0.0, ALU.mult, ALU.add)
                step(ins)
                for r, op in enumerate((ALU.subtract, ALU.add)):
                    tt(turned[0], er, mixed[r], ALU.mult)
                    step(tt(turned[1], ei, mixed[1 - r], ALU.mult))
                    dve.memset(sprev[r][:, :, 0:1], 0.0)
                    tt(sprev[r][:, :, 1:NCH], turned[0][:, :, 0:NCH - 1], turned[1][:, :, 0:NCH - 1], op)
                    step(tt(sfin[:, r, :].unsqueeze(2), turned[0][:, :, NCH - 1:NCH], turned[1][:, :, NCH - 1:NCH], op))
                wait_emptied(dve, ("h0", l, 1))
                h0 = [sprev[r][:, :, NCH:UC] for r in range(2)]
                lam = [x[:, L].unsqueeze(2).to_broadcast([P, NQ, NDEC]) for x in (LBR, LBI)]
                t = [scr[:, r, 0:NQ * NDEC].rearrange("p (q b) -> p q b", q=NQ) for r in range(2)]
                dec = dec[:, 0:2 * NQ * NDEC].rearrange("p (r q b) -> p r q b", r=2, q=NQ)
                for r, op in enumerate((ALU.subtract, ALU.add)):
                    tt(t[0], lam[0], h0[r], ALU.mult)
                    step(tt(t[1], lam[1], h0[1 - r], ALU.mult))
                    step(tt(t[0], t[0], t[1], op))
                    ins = tt(sfin_d[:, r, :, :].rearrange("p b q -> p q b"), t[0], dec[:, r, :, :], ALU.add)
                    if r == 0:
                        step(ins)
                ins.then_inc(emptied["d"], 1)

            def gelu(l):
                for k in range(4):
                    if k == 0:
                        wait_emptied(dve, ("ytd", l))
                    step(dve.tensor_scalar(gel[:, k, :], gel[:, k, :], 0.044715, 1.0, ALU.mult, ALU.add))
                    tt(gel[:, k, :], gel[:, k, :], yT[:, k, :], ALU.mult).then_inc(gelu_arg, 1)
                for k in range(4):
                    dve.wait_ge(gelu_tanh, 4 * l + k + 1)
                    dve.scalar_tensor_tensor(out=yT[:, k, :], in0=gel[:, k, :], scalar=1.0, in1=yT[:, k, :],
                                             op0=ALU.add, op1=ALU.mult).then_inc(y_ready, 1)

            def residual(key, factor):
                for m in range(KD):
                    dve.scalar_tensor_tensor(out=rT[:, m, :], in0=tile_in(dve, (*key, m))[:, 0:T], scalar=factor,
                                             in1=xT[:, m, :], op0=ALU.mult, op1=ALU.add).then_inc(emptied["d"], 1)

            def rsqrt(y, std, v, t):
                step(tt(t, y, y, ALU.mult))
                step(tt(t, t, v, ALU.mult))
                step(dve.tensor_scalar(t, t, -0.5, 1.5, ALU.mult, ALU.add))
                step(tt(y, y, t, ALU.mult))

            def layer_norm(l, which):
                n = 2 * l + which
                mean = tile_in(dve, ("mean", l, which))[:, 0:T].unsqueeze(1).to_broadcast([P, 4, T])
                wait_emptied(dve, ("out", l, KD - 1) if which == 0 else ("down", KD - 1))
                tt(rT[:, 0:4, :], rT[:, 0:4, :], mean, ALU.subtract).then_inc(centred, 1)
                tt(rT[:, 4:8, :], rT[:, 4:8, :], mean, ALU.subtract).then_inc(emptied["d"], 1)
                var = tile_in(dve, ("var", l, which))[:, 0:T]
                dve.wait_ge(std_ready, n + 1)
                dve.reciprocal(std4[:, 2, :], std4[:, 0, :])
                dve.tensor_scalar(std4[:, 1, :], var, EPS, None, ALU.add).then_inc(emptied["d"], 1)
                wait_emptied(dve, ("var", l, which))
                rsqrt(std4[:, 2, :], None, std4[:, 1, :], std4[:, 3, :])
                at = (C_LN1G + KD * l) if which == 0 else C_LN2G
                for k in range(KD):
                    dve.scalar_tensor_tensor(out=rT[:, k, :], in0=rT[:, k, :], scalar=colT[:, at + k:at + k + 1],
                                             in1=std4[:, 2, :], op0=ALU.mult, op1=ALU.mult).then_inc(norm_ready, 1)

            def mixer(l):
                s5_columns(l)
                if l == 0:
                    c_rows(0)
                pooling(l)
                if l == 0:
                    s5_outputs(0)
                    s5_inputs(0)
                    kernel_rows(0)
                states(l)
                for m in range(KD):
                    wait_emptied(dve, ("gate", l, m))
                    dve.scalar_tensor_tensor(out=mT[:, m, :], in0=gates[:, m, :], scalar=1.0,
                                             in1=tile_in(dve, ("pa", l, m))[:, 0:T], op0=ALU.add, op1=ALU.mult)\
                        .then_inc(emptied["d"], 1)
                for i in range(1, NG // 4, 2):
                    to = ytok.rearrange("p j (q h) c -> p h j q c", h=2)[0:UC, 1, :, 2 * (i - 1):2 * (i - 1) + 4, :]
                    dve.tensor_copy(to,
                                    tile_in(dve, ("y", l, i))[0:UC, :].rearrange("p (g j c) -> p j g c", g=4, j=CHUNK))\
                        .then_inc(emptied["d"], 1)
                gelu(l)
                for m in range(4):
                    wait_emptied(dve, ("glu", l, m))
                    dve.scalar_tensor_tensor(out=gel[:, m, :], in0=gel[:, m, :], scalar=1.0, in1=yT[:, m, :],
                                             op0=ALU.add, op1=ALU.mult).then_inc(ob_ready, 1)
                for m in range(KD):
                    wait_emptied(dve, ("gate", l, 8 + m))
                    dve.scalar_tensor_tensor(out=gates[:, 8 + m, :], in0=gates[:, 8 + m, :], scalar=1.0,
                                             in1=tile_in(dve, ("pb", l, m))[:, 0:T], op0=ALU.add, op1=ALU.mult)\
                        .then_inc(emptied["d"], 1)
                    wait_emptied(dve, ("pb", l, m))
                    tt(mT[:, m, :], mT[:, m, :], gates[:, 8 + m, :], ALU.add).then_inc(m_ready, 1)
                residual(("out", l), 0.25 / ALPHA)
                layer_norm(l, 0)

            def dense_ffn():
                for f in range(NFT):
                    wait_emptied(dve, ("fg", f))
                    tt(hT[:, f, :], silu_f[:, f % 2, :], tile_in(dve, ("fu", f))[:, 0:T], ALU.mult)\
                        .then_inc(emptied["d"], 1)
                    if f == 3:
                        c_rows(1)
                    if f == 5:
                        s5_tables(1)
                    if f == 9:
                        s5_outputs(1)
                    if f == 14:
                        s5_inputs(1)
                kernel_rows(1)
                residual(("down",), 1.0 / ALPHA)
                layer_norm(0, 1)

            def routing():
                (LG, EQ, SC, BEST, SECOND, SEL, GATE, POS, WAY, MORE) = route
                (M1, M2, DIFF, EX, DEN, W1, W2, MX) = small3[0], small3[1], small3[2], small3[3], small3[4], small3[5], \
                    small3[6], small3[7]

                def over_e(v):
                    return v.unsqueeze(2).to_broadcast([P, 3, NE])

                step(dve.memset(LG, 0.0))
                dve.wait_ge(router_in, 32)
                dve.wait_ge(const_ready, 11)
                dve.tensor_scalar(WAY, iota[:, 0:NE].unsqueeze(1).to_broadcast([P, 3, NE]), -1.0, float(NE), ALU.mult, ALU.add)
                ps = tile_in(dve, ("logit",))
                tt(LG[:, 0:2, :], ps[:, 0:2 * NE].rearrange("p (h e) -> p h e", e=NE),
                   brt[:, :].unsqueeze(1).to_broadcast([P, 2, NE]), ALU.add)
                tt(LG[0:NDEC, 2, :], ps[0:NDEC, 2 * NE:3 * NE], brt[0:NDEC, :], ALU.add).then_inc(emptied["d"], 1)
                wait_emptied(dve, ("logit",))
                for m, one in ((M1, BEST), (M2, SECOND)):
                    step(dve.tensor_reduce(m, LG, AX.X, ALU.max))
                    step(tt(EQ, LG, over_e(m), ALU.is_equal))
                    step(tt(SC, EQ, WAY, ALU.mult))
                    step(dve.tensor_reduce(MX, SC, AX.X, ALU.max))
                    step(tt(one, SC, over_e(MX), ALU.is_equal))
                    if one is BEST:
                        step(dve.scalar_tensor_tensor(out=LG, in0=BEST, scalar=-3.0e38, in1=LG, op0=ALU.mult, op1=ALU.add))
                tt(SEL, BEST, SECOND, ALU.add).then_inc(sel_ready, 1)
                tt(DIFF, M2, M1, ALU.subtract).then_inc(rexp_arg, 1)
                dve.wait_ge(rexp_ready, 1)
                step(dve.tensor_scalar(DEN, EX, 1.0, None, ALU.add))
                step(dve.reciprocal(W1, DEN))
                step(tt(W2, EX, W1, ALU.mult))
                tt(BEST, BEST, over_e(W1), ALU.mult)
                step(tt(SECOND, SECOND, over_e(W2), ALU.mult))
                step(tt(GATE, BEST, SECOND, ALU.add))
                for i in range(6):
                    h, half = i // 2, i % 2
                    m = TILES[h][1]
                    wait_emptied(dve, ("xtok", i))
                    dve.tensor_copy(acc[0:m, h, 512 * half:512 * half + 512], xtok[0:m, h, 512 * half:512 * half + 512])
                ps = tile_in(dve, ("pos",))
                step(dve.memset(POS, 0.0))
                dve.tensor_copy(POS[:, 0:2, :], ps[:, 0:2 * NE].rearrange("p (h e) -> p h e", e=NE))
                dve.tensor_copy(POS[0:NDEC, 2, :], ps[0:NDEC, 2 * NE:3 * NE])
                step(dve.tensor_reduce(MX[:, 0:1], ps[:, 3 * NE:4 * NE], AX.X, ALU.max))
                step(dve.tensor_scalar(DEN[:, 0:1], MX[:, 0:1], float(P), float(NE), ALU.is_gt, ALU.mult))
                step(dve.tensor_scalar(DEN[:, 1:2], MX[:, 0:1], float(2 * P), float(NE), ALU.is_gt, ALU.mult))
                step(tt(DEN[:, 0:1], DEN[:, 0:1], DEN[:, 1:2], ALU.add))
                dve.tensor_scalar(npass_i[0:1, 0:1], DEN[0:1, 0:1], float(NE), None, ALU.add).then_inc(npass_ready, 1)
                dve.memset(pos_of, -1.0)
                dve.memset(sel_of, 0.0)
                step(dve.memset(gate_of, 0.0))
                for c in range(3):
                    at = slice(NE * c, NE * c + NE)
                    dve.tensor_scalar(pos_of[:, :, at], POS, float(-P * c), None, ALU.add)
                    dve.tensor_copy(sel_of[:, :, at], SEL)
                    ins = dve.tensor_copy(gate_of[:, :, at], GATE)
                ins.then_inc(emptied["d"], 1)
                wait_emptied(dve, ("pos",))

            def slots(out, weight, i, ready):
                for h, (_, m) in enumerate(TILES):
                    ins = dve.tensor_scalar(out[0:m, h, :], iota[0:m, :], pos_of[0:m, h, bass.ds(i, 1)],
                                            weight[0:m, h, bass.ds(i, 1)], ALU.is_equal, ALU.mult)
                ins.then_inc(ready, 1)

            def one_pass(i):
                wait_pass_emptied(dve, ("spread",), i, back=1)
                slots(pickg, gate_of, i, pickg_ready)
                for f in range(NFC):
                    wait_pass_emptied(dve, ("g", f), i)
                    wait_pass_emptied(dve, ("hT", (f - 2) % NFC), i, back=int(f < 2))
                    tt(hid_e[f % 2], silu_e[f % 2], pass_tile_in(dve, ("u", f), i)[:, :], ALU.mult)\
                        .then_inc(emptied["d"], 1)
                    if f == 2:
                        slots(pick, sel_of, i + 1, pick_ready)
                dve.tensor_copy(xg[:, 4:8, :], pass_tile_in(dve, ("gather", 1), i)[:, :]
                                .rearrange("p (k s) -> p k s", k=4)).then_inc(emptied["d"], 1)
                dve.tensor_scalar(y_e[:, 512:1024], pass_tile_in(dve, ("ye", 1), i)[:, :], 1.0 / ALPHA, None, ALU.mult)\
                    .then_inc(emptied["d"], 1)
                for s in range(6):
                    h, half = s // 2, s % 2
                    m = TILES[h][1]
                    part_ = acc[0:m, h, 512 * half:512 * half + 512]
                    tt(part_, part_, pass_tile_in(dve, ("scatter", s), i)[0:m, :], ALU.add).then_inc(emptied["d"], 1)

            def final_norm(n_done):
                VAR, STD, Y, TMP = small3[10], small3[11], small3[12], small3[13]
                dve.wait_ge(emptied["d"], n_done)
                step(dve.memset(mv, 1.0))
                for h, (_, m) in enumerate(TILES):
                    for half in range(2):
                        ins = dve.bn_stats(stats[0:m, h, 6 * half:6 * half + 6], acc[0:m, h, 512 * half:512 * half + 512])
                    step(ins)
                    step(dve.bn_aggr(mv[0:m, h, :], stats[0:m, h, :]))
                dve.tensor_scalar(VAR, mv[:, :, 1], EPS, None, ALU.add).then_inc(fvar_ready, 1)
                dve.wait_ge(fstd_ready, 1)
                step(dve.reciprocal(Y, STD))
                rsqrt(Y, None, VAR, TMP)
                dve.wait_ge(lnb_in, 32)
                for h, (_, m) in enumerate(TILES):
                    row = acc[0:m, h, :]
                    step(dve.tensor_scalar(row, row, mv[0:m, h, 0:1], Y[0:m, h:h + 1], ALU.subtract, ALU.mult))
                    step(tt(row, row, lnb[0:m, 0, :], ALU.mult))
                    tt(row, row, lnb[0:m, 1, :], ALU.add).then_inc(y_out, 1)

            angles()
            s5_tables(0)
            mixer(0)
            dense_ffn()
            mixer(1)
            routing()
            slots(pick, sel_of, 0, pick_ready)
            dve.tensor_copy(xg[:, 4:8, :], tile_in(dve, ("gather0", 1))[:, :].rearrange("p (k s) -> p k s", k=4))\
                .then_inc(emptied["d"], 1)
            dve.wait_ge(npass_ready, 1)
            npass = dve.value_load(npass_i[0:1, 0:1], min_val=NE, max_val=MAXPASS)
            with dve.Fori(0, npass) as i:
                one_pass(i)
            final_norm(npass * per_pass.count["d"] + tiles.count["d"])

        @block.tensor
        def _(pe):
            owed = [0]

            def mm(out, lhsT, rhs, start, stop, signal=None):
                ins = pe.matmul(out, lhsT, rhs, start=start, stop=stop, skip_group_check=True)
                if signal is not None:
                    ins.then_inc(signal, 1)
                elif owed[0]:
                    ins.then_inc(used, 1)
                    owed[0] = 0
                return ins

            def turn_over(out, in_, n, signal=None, at=0):
                ins = pe.transpose(out, in_, ident[at:at + n, at:at + n])
                if signal is not None:
                    ins.then_inc(signal, 1)
                elif owed[0]:
                    ins.then_inc(used, 1)
                    owed[0] = 0

            def claim(key):
                i = tiles.filled[key] - 1
                if i >= NBANK:
                    wait_emptied(pe, tiles.keys[i - NBANK])
                return bank[tiles.bank[key]]

            def slot(key):
                i = slot_of[key]
                _, _, k, n = plan[i]
                pe.wait_ge(landed[i % RING], 16 * (i // RING + 1))
                return ring[i % RING][:, 0:k * n].rearrange("p (k n) -> p k n", k=k)

            def through(signal_given):
                if signal_given is None:
                    return used
                assert not owed[0]
                owed[0] = 1
                return signal_given

            def project(names, slots_, rhs, ready=None):
                for m, name in enumerate(names):
                    ps = claim(name)
                    k = 0
                    n_k = sum(plan[slot_of[s]][2] for s in slots_)
                    for s in slots_:
                        wt = slot(s)
                        for kk in range(wt.shape[1]):
                            if ready and m == 0:
                                ready(k)
                            end_tile, end_slot = k == n_k - 1, kk == wt.shape[1] - 1 and m == len(names) - 1
                            sig = filled if end_tile else None
                            if end_slot:
                                sig = through(sig)
                            mm(ps[:, 0:T], wt[:, kk, P * m:P * m + P], rhs[:, k, :], k == 0, end_tile, sig)
                            k += 1

            def stream(l):
                if l == 0:
                    return lambda k: wait_emptied(pe, ("x", k))
                return lambda k: pe.wait_ge(x_next, KD + k + 1)

            def c_transposed(l):
                pe.wait_ge(layer_in, 16 * LAYER_DMAS * (l + 1))
                for r in range(2):
                    ps = claim(("ct", l, r))
                    for k in range(4):
                        turn_over(ps[:, P * k:P * k + P], cnat[:, r, k, :, :], P, filled if k == 3 else None)

            def s5_matrices(l):
                pe.wait_ge(w1n_ready, l + 1)
                for r in range(2):
                    for i in range(4):
                        ps = claim(("w1t", l, r, i))
                        for q in range(4):
                            turn_over(ps[:, P * q:P * q + P], w1n[r][:, 4 * i + q, :, :], P, filled if q == 3 else None)
                pe.wait_ge(vmat_ready, l + 1)
                for i in range(NG // 4):
                    ps = claim(("kern", l, i))
                    at = NS * (i % 2)
                    for n in range(4):
                        q = 4 * (i // 2) + n
                        for r in range(2):
                            mm(ps[0:GC, P * n:P * n + P], bbar[at:at + NS, r, q, :],
                               vmat[r][at:at + NS, q, 0:CHUNK, :], r == 0, r == 1, filled if n == 3 and r == 1 else None)

            def mixer(l):
                for h, (at, m) in enumerate(TILES):
                    ps = claim(("ub", l, h))
                    for k in range(KD):
                        if h == 0:
                            stream(l)(k)
                        wt = slot(("ub", l, k // 4))
                        sig = filled if k == KD - 1 else None
                        if h == 2 and k % 4 == 3:
                            sig = through(sig)
                        mm(ps[0:m, :], xT[:, k, at:at + m], wt[:, k % 4, :], k == 0, k == KD - 1, sig)
                project([("ua", l, m) for m in range(4)], [("ua", l, h) for h in range(2)], xT)
                if l == 0:
                    c_transposed(0)
                wait_emptied(pe, ("ub", l, 2))
                for i in range(3):
                    ps = claim(("ut", l, i))
                    a, b = 12 * i, min(12 * i + 12, NG)
                    for g in range(a, b):
                        turn_over(ps[:, UC * (g - a):UC * (g - a) + UC], utok[0:UC, g, :, :], UC,
                                  filled if g == b - 1 else None)
                pe.wait_ge(layer_in, 16 * LAYER_DMAS * (l + 1))
                pe.wait_ge(const_ready, 9)
                ps = claim(("pd", l))
                for g in range(4):
                    mm(ps[:, NDEC * g:NDEC * g + NDEC], spool[:, P * g:P * g + P], pmask[:, g, :], True, True,
                       filled if g == 3 else None)
                for n in range(4):
                    project([("gate", l, 4 * n + m) for m in range(4)], [("gate", l, n, h) for h in range(2)], xT)
                for r in range(2):
                    turn_over(claim(("h0", l, r))[:, 0:P], h0n[:, r, :], P, filled)
                wait_emptied(pe, ("ua", l, 3))
                ps = claim(("rows", l, 0))
                for g in range(4):
                    turn_over(ps[0:PSTATE, P * g:P * g + P], pext[:, g, WX - PSTATE:WX], P, filled if g == 3 else None)
                ps = claim(("rows", l, 1))
                for g in range(4):
                    turn_over(ps[0:NDEC, P * g:P * g + P], udec[:, g, :], P, filled if g == 3 else None)
                if l == 0:
                    s5_matrices(0)
                wait_emptied(pe, ("w1t", l, 1, 3))
                wait_emptied(pe, ("ut", l, 2))
                for r in range(2):
                    ps = claim(("chunk", l, r))
                    for g in range(NG):
                        q, at = g // 2, NS * (g % 2)
                        mm(ps[at:at + NS, NCH * q:NCH * q + NCH], w1T[r][:, q, at:at + NS], ucol[:, g, 0:NCH],
                           True, True, filled if g == NG - 1 else None)
                ps = claim(("chunk", l, 2))
                for r in range(2):
                    for g in range(NG):
                        q, at = g // 2, NS * (g % 2)
                        c = NDEC * (NQ * r + q)
                        mm(ps[at:at + NS, c:c + NDEC], w1T[r][P - 32:P, q, at:at + NS], ucol[P - 32:P, g, NCH:UC],
                           True, True, filled if r == 1 and g == NG - 1 else None)
                wait_emptied(pe, ("pd", l))
                wt = slot(("wpool", l))
                for g in range(4):
                    sig = through(filled) if g == 3 else filled
                    mm(claim(("mix", l, g))[:, 0:T], wt[:, g, :], poolT[:, g, :], True, True, sig)
                for h in range(2):
                    project([("pa", l, 4 * h + m) for m in range(4)], [("pa", l, h)], oaT,
                            lambda k: wait_emptied(pe, ("mix", l, k)))
                pe.wait_ge(toep_ready, 16 * CHUNK * (l + 1))
                wait_emptied(pe, ("chunk", l, 2))
                for i in range(NG // 4):
                    ps = claim(("y", l, i))
                    half = i % 2
                    at = NS * half
                    qs = range(4 * (i // 2), 4 * (i // 2) + 4)
                    for n, q in enumerate(qs):
                        mm(ps[0:UC, P * n:P * n + P], ucol[:, 2 * q + half, :], toep[:, 2 * q + half, :], n == 0, False)
                    for n, q in enumerate(qs):
                        for r in range(2):
                            mm(ps[0:UC, P * n:P * n + P], sprev[r][at:at + NS, q, :], vmat[r][at:at + NS, q, 1:NPOW, :],
                               False, n == 3 and r == 1, filled if n == 3 and r == 1 else None)
                wait_emptied(pe, ("y", l, NG // 4 - 2))
                wait_emptied(pe, ("y", l, NG // 4 - 1))
                for k in range(4):
                    ps = claim(("yt", l, k))
                    for j in range(CHUNK):
                        turn_over(ps[:, NCH * j:NCH * j + NCH], ytok[0:NCH, j, 8 * k:8 * k + 8, :], NCH,
                                  filled if j == CHUNK - 1 else None)
                ps = claim(("ytd", l))
                for k in range(4):
                    turn_over(ps[:, NDEC * k:NDEC * k + NDEC], ytok[NCH:UC, 0, 8 * k:8 * k + 8, :], NDEC,
                              filled if k == 3 else None, NCH)
                ps = claim(("state", l))
                for r in range(2):
                    turn_over(ps[0:NQ, P * r:P * r + P], sfin[:, r, :], P, filled if r else None)
                ps = claim(("stated", l))
                for r in range(2):
                    turn_over(ps[:, P * r:P * r + P], sfin_d[:, r, :, :], P,
                              filled if r else None)
                project([("glu", l, m) for m in range(4)], [("glu", l)], yT, lambda k: pe.wait_ge(y_ready, 4 * l + k + 1))
                for h in range(2):
                    project([("pb", l, 4 * h + m) for m in range(4)], [("pb", l, h)], gel,
                            lambda k: pe.wait_ge(ob_ready, 4 * l + k + 1))
                for n in range(4):
                    project([("out", l, 2 * n + m) for m in range(2)], [("out", l, n)], mT,
                            lambda k: pe.wait_ge(m_ready, KD * l + k + 1))
                layer_norm(l, 0)

            def layer_norm(l, which):
                n = 2 * l + which
                ps = claim(("mean", l, which))
                for k in range(KD):
                    wait_emptied(pe, ("out", l, k) if which == 0 else ("down", k))
                    mm(ps[:, 0:T], avg[:, :], rT[:, k, :], k == 0, k == KD - 1, filled if k == KD - 1 else None)
                ps = claim(("var", l, which))
                for k in range(KD):
                    pe.wait_ge(squared, 2 * n + k // 4 + 1)
                    mm(ps[:, 0:T], avg[:, :], mT[:, k, :], k == 0, k == KD - 1, filled if k == KD - 1 else None)

            def dense_ffn():
                for c in range(NFT // 2):
                    for m in range(2):
                        f = 2 * c + m
                        for name, s in (("fg", "w_ffn_gate"), ("fu", "w_ffn_up")):
                            ps = claim((name, f))
                            wt = slot((s, c))
                            for k in range(KD):
                                if f == 0:
                                    pe.wait_ge(x_next, k + 1)
                                sig = filled if k == KD - 1 else None
                                if k == KD - 1 and m == 1:
                                    sig = through(sig)
                                mm(ps[:, 0:T], wt[:, k, P * m:P * m + P], xT[:, k, :], k == 0, k == KD - 1, sig)
                        if f == 3:
                            c_transposed(1)
                s5_matrices(1)
                for n in range(4):
                    ps = [claim(("down", 2 * n + m)) for m in range(2)]
                    for a in range(0, NFT, 8):
                        wt = slot(("down", n, a))
                        for m in range(2):
                            for kk in range(wt.shape[1]):
                                f = a + kk
                                if n == 0 and m == 0:
                                    wait_emptied(pe, ("fu", f))
                                sig = filled if f == NFT - 1 else None
                                if m == 1 and kk == wt.shape[1] - 1:
                                    sig = through(sig)
                                mm(ps[m][:, 0:T], wt[:, kk, P * m:P * m + P], hT[:, f, :], f == 0, f == NFT - 1, sig)
                layer_norm(0, 1)

            pe.wait_ge(const_ready, 1)
            pe.wait_ge(prm_in, 16 * 11)
            pe.wait_ge(prm_rows, 1)
            ps = claim(("prm",))
            turn_over(ps[:, 0:96], prm, 96)
            turn_over(ps[:, 96:208], cols, C_END)
            turn_over(ps[0:GC, 208:272], dsk, DEPTH * NG, filled)
            pe.wait_ge(x_in, 16 * 9)
            for k in range(KD):
                ps = claim(("x", k))
                for h, (at, m) in enumerate(TILES):
                    turn_over(ps[:, at:at + m], xstage[0:m, h, P * k:P * k + P], m, filled if h == 2 else None)
            mixer(0)
            dense_ffn()
            mixer(1)

            pe.wait_ge(router_in, 32)
            ps = claim(("logit",))
            for h, (at, m) in enumerate(TILES):
                for k in range(KD):
                    if h == 0:
                        pe.wait_ge(x_next, 2 * KD + k + 1)
                    mm(ps[0:m, NE * h:NE * h + NE], xT[:, k, at:at + m], wrt[:, k, :], k == 0, k == KD - 1,
                       filled if h == 2 and k == KD - 1 else None)
            for i in range(6):
                h, half = i // 2, i % 2
                at, m = TILES[h]
                ps = claim(("xtok", i))
                for kk in range(4):
                    turn_over(ps[0:m, P * kk:P * kk + P], xT[:, 4 * half + kk, at:at + m], P, filled if kk == 3 else None)
            pe.wait_ge(sel_ready, 1)
            pe.wait_ge(const_ready, 11)
            ps = claim(("pos",))
            for h in range(4):
                m = TILES[h][1] if h < 3 else P
                for hh in range(min(h + 1, 3)):
                    mk = TILES[hh][1]
                    mat = tri if hh == h else ones
                    mm(ps[0:m, NE * h:NE * h + NE], mat[0:mk, 0:m], route[5][0:mk, hh, :], hh == 0, hh == min(h, 2),
                       filled if h == 3 and hh == 2 else None)

            def gather(banks):
                for k in range(KD):
                    for h, (_, m) in enumerate(TILES):
                        mm(banks[k // 4][:, P * (k % 4):P * (k % 4) + P], xtok[0:m, h, P * k:P * k + P],
                           pick[0:m, h, :], h == 0, h == 2, filled if k % 4 == 3 and h == 2 else None)

            wait_emptied(pe, ("xtok", 5))
            pe.wait_ge(pick_ready, 1)
            gather([claim(("gather0", i)) for i in range(2)])
            for owner in "ad":
                pe.wait_ge(emptied[owner], tiles.count[owner])

            def claim_in_pass(key, i):
                b = pass_bank[key]
                same = [k for k in per_pass.keys if pass_bank[k] == b]
                at = same.index(key)
                wait_pass_emptied(pe, same[at - 1], i, back=int(at == 0))
                return bank[b]

            def expert_slot(what, f, h, i):
                s = n_plan + PASS_SLOTS.index((what, f, h))
                pe.wait_ge(landed[s % RING], i * (16 * PER_PASS // RING) + 16 * (s // RING + 1))
                k = 2 if what == "down" else 4
                return ring[s % RING][:, :].rearrange("p (k n) -> p k n", k=k)

            def one_pass(i):
                def gate_up(f):
                    for name, what in (("g", "gate"), ("u", "up")):
                        ps = claim_in_pass((name, f), i)
                        for h in range(2):
                            wt = expert_slot(what, f, h, i)
                            for kk in range(4):
                                k = 4 * h + kk
                                sig = filled if k == KD - 1 else None
                                if kk == 3:
                                    sig = through(sig)
                                mm(ps[:, :], xg[:, k, :], wt[:, kk, :], k == 0, k == KD - 1, sig)

                def hidden_transposed(f):
                    wait_pass_emptied(pe, ("u", f), i)
                    ps = claim_in_pass(("hT", f), i)
                    for n in range(4):
                        turn_over(ps[:, P * n:P * n + P], hid_e[f % 2][:, P * n:P * n + P], P, filled if n == 3 else None)

                def down(f):
                    if f == 0:
                        for n in range(2):
                            claim_in_pass(("ye", n), i)
                    wait_pass_emptied(pe, ("hT", f), i)
                    for h in range(2):
                        wt = expert_slot("down", f, h, i)
                        for kk in range(2):
                            for n in range(2):
                                k = 2 * h + kk
                                end = f == NFC - 1 and k == 3
                                sig = filled if end else None
                                if kk == 1 and n == 1:
                                    sig = through(sig)
                                mm(bank[4 + n][:, :], hidT_e[f % 2][:, k, :], wt[:, kk, 512 * n:512 * n + 512],
                                   f == 0 and k == 0, end, sig)

                for n in range(2):
                    wait_pass_emptied(pe, ("gather", n), i, back=1)
                for f in range(NFC + 1):
                    if f < NFC:
                        gate_up(f)
                    if f == 0:
                        pe.wait_ge(pickg_ready, i + 1)
                        ps = claim_in_pass(("spread",), i)
                        for h, (at, m) in enumerate(TILES):
                            turn_over(ps[:, at:at + m], pickg[0:m, h, :], m, filled if h == 2 else None)
                    if f == NFC:
                        pe.wait_ge(pick_ready, i + 2)
                        gather([claim_in_pass(("gather", n), i) for n in range(2)])
                    if f > 0:
                        hidden_transposed(f - 1)
                        down(f - 1)
                wait_pass_emptied(pe, ("spread",), i)
                for s in range(6):
                    h, half = s // 2, s % 2
                    at, m = TILES[h]
                    wait_pass_emptied(pe, ("ye", half), i)
                    ps = claim_in_pass(("scatter", s), i)
                    if s == 0:
                        mm(ps[0:m, 0:256], spread[:, at:at + m], y_e[:, 0:256], True, True)
                        mm(ps[0:m, 256:512], spread[:, at:at + m], y_e[:, 256:512], True, True, filled)
                    else:
                        mm(ps[0:m, :], spread[:, at:at + m], y_e[:, 512 * half:512 * half + 512], True, True, filled)
                assert not owed[0]

            with all_passes(pe) as i:
                one_pass(i)


_OUTS = [(1, SEQ, D), (NDEC, 1, D), (DEPTH, 1, PSTATE, PW), (DEPTH, 1, NG, NS), (DEPTH, 1, NG, NS),
         (DEPTH, NDEC, PSTATE, PW), (DEPTH, NDEC, NG, NS), (DEPTH, NDEC, NG, NS)]


def kernel(**inputs):
    import numpy as _np
    import concourse.bacc as _bacc
    from concourse.bass_utils import run_bass_kernel_spmd as _run

    nc = _bacc.Bacc("TRN2", target_bir_lowering=False, num_devices=1)
    arrays, args = {}, {}
    for name, x in inputs.items():
        a = _np.ascontiguousarray(x)
        arrays[f"in_{name}_dram"] = a
        args[name] = nc.dram_tensor(f"in_{name}_dram", a.shape, F32, kind="ExternalInput").ap()
    outs = [nc.dram_tensor(f"out_{i}_dram", s, F32, kind="ExternalOutput").ap() for i, s in enumerate(_OUTS)]
    trunk_kernel(nc, args, outs)
    r = _run(nc, [arrays], core_ids=[0])
    return tuple(r.results[0][f"out_{i}_dram"] for i in range(len(_OUTS)))
```

```python
import math
from contextlib import ExitStack

import concourse.bass as bass
from concourse import mybir

F32 = mybir.dt.float32
F32R = mybir.dt.float32r
I32 = mybir.dt.int32
ALU = mybir.AluOpType
ACT = mybir.ActivationFunctionType
AX = mybir.AxisListType

P = 128
D = 1024
KD = D // P
SEQ = 256
NDEC = 8
T = SEQ + NDEC
TILES = ((0, P), (P, P), (2 * P, NDEC))
DEPTH = 2
CHUNK = 8
NCH = SEQ // CHUNK
UC = NCH + NDEC
PW = 512
WINDOWS = (2, 4, 8, 16)
PSTATE = max(WINDOWS) - 1
PAD = PSTATE + 1
SW = 512
NG = 32
GC = SW // NG
NS = 64
NQ = NG * NS // P
NPOW = CHUNK + 1
FF = 11 * D // 4
NFT = FF // P
NE = 8
FE = 7 * D // 2
FCH = 512
NFC = FE // FCH
ALPHA = (2.0 * DEPTH) ** 0.25
EPS = 1e-5 / ALPHA ** 2
RING = 6
PAIRS = 3
SLOT = 2048
MAGIC = 12582912.0
TWO_PI = (6.28125, 0.0019350051879882812, 2 * math.pi - 6.28125 - 0.0019350051879882812)
PI_SAFE = 3.1415925
NBANK = 8
MAXPASS = 3 * NE
C_BIN, C_LN1G, C_LN1B, C_LN2G, C_LN2B, C_PS, C_BG, C_END = 0, 48, 64, 80, 88, 96, 104, 112


def weight_plan(w):
    plan = []

    def add(key, src, k, n):
        plan.append((key, src.rearrange("(k p) n -> p k n", p=P) if len(src.shape) == 2 else src, k, n))

    for l in range(DEPTH):
        win = w["w_in"][l]
        for key, at in [(("ub", l), PW), (("ua", l), 0)] + [(("gate", l, n), PW + SW + 512 * n) for n in range(4)]:
            for h in range(2):
                add((*key, h), win[512 * h:512 * h + 512, at:at + 512], 4, 512)
        add(("wpool", l), w["w_pool"][l].rearrange("g c d -> c g d"), 4, P)
        for h in range(2):
            add(("pa", l, h), w["w_proj_a"][l][:, 512 * h:512 * h + 512], 4, 512)
        add(("glu", l), w["w_glu"][l], 4, 512)
        for h in range(2):
            add(("pb", l, h), w["w_proj_b"][l][:, 512 * h:512 * h + 512], 4, 512)
        for m in range(4):
            add(("out", l, m), w["w_out"][l][:, 256 * m:256 * m + 256], 8, 256)
        if l == 0:
            for c in range(NFT // 2):
                for name in ("w_ffn_gate", "w_ffn_up"):
                    add((name, c), w[name][0][:, 256 * c:256 * c + 256], 8, 256)
            for m in range(4):
                for a in range(0, NFT, 8):
                    b = min(a + 8, NFT)
                    add(("down", m, a), w["w_ffn_down"][0][P * a:P * b, 256 * m:256 * m + 256], b - a, 256)
    return plan


PASS_SLOTS = []
for _f in range(NFC + 1):
    if _f < NFC:
        PASS_SLOTS += [("gate", _f, 0), ("gate", _f, 1), ("up", _f, 0), ("up", _f, 1)]
    if _f > 0:
        PASS_SLOTS += [("down", _f - 1, 0), ("down", _f - 1, 1)]
PER_PASS = len(PASS_SLOTS)


def psum_plan():
    tiles = [(("x", k), "ad"[k % 2]) for k in range(KD)]

    def s5_matrices(l):
        return ([(("w1t", l, r, i), "a") for r in range(2) for i in range(4)]
                + [(("kern", l, i), "d") for i in range(NG // 4)])

    for l in range(DEPTH):
        ub = [(("ub", l, h), "d") for h in range(3)]
        tiles += [(("prm",), "d")] + ub if l == 0 else ub
        tiles += [(("ua", l, m), "a") for m in range(4)]
        if l == 0:
            tiles += [(("ct", l, r), "d") for r in range(2)]
        tiles += [(("ut", l, i), "a") for i in range(3)] + [(("pd", l), "d")]
        tiles += [(("gate", l, m), "a") for m in range(16)]
        tiles += [(("h0", l, r), "a") for r in range(2)] + [(("rows", l, s), "a") for s in range(2)]
        if l == 0:
            tiles += s5_matrices(l)
        tiles += [(("chunk", l, r), "d") for r in range(3)] + [(("mix", l, g), "a") for g in range(4)]
        tiles += [(("pa", l, m), "d") for m in range(KD)]
        tiles += [(("y", l, i), "ad"[i % 2]) for i in range(NG // 4)]
        tiles += [(("yt", l, k), "a") for k in range(4)] + [(("ytd", l), "a"), (("state", l), "a"), (("stated", l), "a")]
        tiles += [(("glu", l, m), "a") for m in range(4)]
        tiles += [(("pb", l, m), "d") for m in range(KD)] + [(("out", l, m), "d") for m in range(KD)]
        tiles += [(("mean", l, 0), "d"), (("var", l, 0), "d")]
        if l == 0:
            for f in range(NFT):
                tiles += [(("fg", f), "a"), (("fu", f), "d")]
                if f == 3:
                    tiles += [(("ct", 1, r), "d") for r in range(2)]
            tiles += s5_matrices(1)
            tiles += [(("down", m), "d") for m in range(KD)] + [(("mean", l, 1), "d"), (("var", l, 1), "d")]
    tiles += [(("logit",), "d"), (("logits",), "d")] + [(("xtok", i), "a") for i in range(6)] + [(("pos",), "d")]
    tiles += [(("gather0", 0), "d"), (("gather0", 1), "d")]
    return tiles


class Tiles:

    def __init__(self, tiles):
        self.keys = [k for k, _ in tiles]
        self.filled = {k: i + 1 for i, (k, _) in enumerate(tiles)}
        count = {"a": 0, "d": 0}
        self.emptied = {}
        for k, owner in tiles:
            count[owner] += 1
            self.emptied[k] = (owner, count[owner])
        self.count = count
        self.bank = {k: i % NBANK for i, k in enumerate(self.keys)}


PASS_TILES = [(("scatter", _s), "d", (7, 6, 4, 5)[_s % 4]) for _s in range(6)]
for _f in range(NFC):
    PASS_TILES += [(("g", _f), "a", 2 * (_f % 2)),
                   (("hT", _f - 1), "d", 6 + (_f - 1) % 2) if _f > 0 else (("spread",), "a", 7),
                   (("u", _f), "d", 2 * (_f % 2) + 1)]
PASS_TILES += [(("hT", NFC - 1), "d", 6 + (NFC - 1) % 2), (("gather", 0), "d", 2), (("gather", 1), "d", 3)]
PASS_TILES += [(("ye", 0), "a", 4), (("ye", 1), "d", 5)]


def trunk_kernel(nc, w, outs):
    y_prompt, y_sample, pool_p, re_p, im_p, pool_s, re_s, im_s = outs
    plan = weight_plan(w)
    n_plan = len(plan)
    slot_of = {key: i for i, (key, _, _, _) in enumerate(plan)}
    tiles = Tiles(psum_plan())
    per_pass = Tiles([(k, owner) for k, owner, _ in PASS_TILES])
    pass_bank = {k: b for k, _, b in PASS_TILES}
    assert PER_PASS % RING == 0

    with ExitStack() as ctx:
        def sb(name, shape, dt=F32):
            return ctx.enter_context(nc.sbuf_tensor(name, shape, dt))

        def sem(name):
            return ctx.enter_context(nc.semaphore(name))

        ring = [sb(f"weights{i}", [P, SLOT]) for i in range(RING)]
        WORK = 8 * 1024 + 2 * NQ * NPOW * GC
        prod_size = NQ * NPOW * GC
        ssm = sb("ssm", [P, WORK + 4096 + 2 * NG * UC])
        prmT = sb("prmT", [P, 96])
        colT = sb("colT", [P, C_END])
        colH = sb("colH", [P, C_END])
        colD = sb("colD", [P, 8])
        dskT = sb("dskT", [GC, DEPTH * NG])
        tiny = sb("tiny", [P, 20, DEPTH * NQ])
        powv = sb("powv", [P, 2, NQ, CHUNK])
        scr = sb("scr", [P, 2, NQ * NCH // 2])
        ident = sb("ident", [P, P])
        tri = sb("tri", [P, P])
        ones = sb("ones", [P, P])
        avg = sb("avg", [P, P])
        iota = sb("iota", [P, P])
        pmask = sb("pmask", [NDEC * PSTATE, 4, NDEC])
        rcount = sb("rcount", [P, 4, PAD])
        udec = sb("udec", [P, 4, NDEC])
        pdec = sb("pdec", [P, 4, NDEC])
        pfix = sb("pfix", [P, PAD])
        srow = sb("srow", [P, 2, P])
        srow_p = sb("srow_p", [NQ, 2, P])
        sfin = sb("sfin", [P, 2, NQ])
        sfin_d = sb("sfin_d", [P, 2, NDEC, NQ])
        consts = sb("consts", [P, 4])
        npass_i = sb("npass_i", [1, 1], I32)
        wrt = sb("wrt", [P, KD, NE])
        brt = sb("brt", [P, NE])
        rows_d = sb("rows_d", [NDEC, PW])
        with ExitStack() as early:
            def sb_early(name, shape):
                return early.enter_context(nc.sbuf_tensor(name, shape, F32))

            bnat = sb_early("bnat", [P, 2, NQ, GC])
            bbar = sb_early("bbar", [P, 2, NQ, GC])
            cnat = sb_early("cnat", [P, 2, 4, 2, NS])
            ctr = sb_early("ctr", [P, 2, NQ, GC])
            h0n = sb_early("h0n", [P, 2, P])
            spool = sb_early("spool", [NDEC * PSTATE, PW])
            powr = sb_early("powr", [P, 2, NQ, NPOW])
            turn = sb_early("turn", [P, 2, NQ, NCH])
            decay = sb_early("decay", [P, NQ, NCH])
            ubias = sb_early("ubias", [P, SW])
            xT = sb_early("xT", [P, KD, T])
            r_all = sb_early("r_all", [P, max(KD * T, prod_size)])
            wide = sb_early("wide", [P, 25 * T])
        w_hi = [sb(f"w_hi{i}", [P, SLOT], F32R) for i in range(PAIRS)]
        w_lo = [sb(f"w_lo{i}", [P, SLOT], F32R) for i in range(PAIRS)]
        xg_hi = sb("xg_hi", [P, KD, P], F32R)
        xg_lo = sb("xg_lo", [P, KD, P], F32R)
        hidT_hi = [sb(f"hidT_hi{i}", [P, 4, P], F32R) for i in range(2)]
        hidT_lo = [sb(f"hidT_lo{i}", [P, 4, P], F32R) for i in range(2)]
        rT = r_all[:, 0:KD * T].rearrange("p (k t) -> p k t", k=KD)
        wide_t = wide[:, :].rearrange("p (k t) -> p k t", k=25)
        gates = wide_t[:, 0:16, :]
        mT = wide_t[:, 16:24, :]
        hT = wide_t[:, 0:NFT, :]
        prod = r_all[:, 0:prod_size]
        xstage = wide[:, 0:3 * D].rearrange("p (h n) -> p h n", h=3)
        poolT = wide_t[:, 16:20, :]
        WX = PAD + SEQ
        pext = wide[:, 20 * T:20 * T + 4 * WX].rearrange("p (g t) -> p g t", g=4)
        win_a = r_all[:, 0:4 * WX].rearrange("p (g t) -> p g t", g=4)
        win_b = r_all[:, 4 * WX:7 * WX].rearrange("p (g t) -> p g t", g=3)
        oaT = rT[:, 0:4, :]
        yT = rT[:, 4:8, :]


        def part(a, pattern=None, **kw):
            n = 1
            for x in kw.pop("of"):
                n *= x
            v = ssm[:, a:a + n]
            return v.rearrange(pattern, **kw) if pattern else v

        def block3(a, x, y, z=None):
            if z is None:
                return part(a, "p (x y) -> p x y", x=x, of=(x, y))
            return part(a, "p (x y z) -> p x y z", x=x, y=y, of=(x, y, z))

        toep = block3(0, NG, P)
        w1T = [block3(4096 + 2048 * r, NQ, P) for r in range(2)]
        vmat = [block3(8192 + 2304 * r, NQ, NPOW, GC) for r in range(2)]
        w1n = [block3(WORK + 2048 * r, NQ, CHUNK, GC) for r in range(2)]
        kern = block3(WORK, NG, P)
        utok = block3(WORK, NG, CHUNK, GC)
        ytok = block3(WORK, CHUNK, NG, GC)
        ucol = block3(WORK + 4096, NG, UC)
        sprev = [block3(WORK + 4096 + NG * UC + NQ * UC * r, NQ, UC) for r in range(2)]
        turned = [r_all[:, 4 * T + 512 * r:4 * T + 512 * r + 512].rearrange("p (q c) -> p q c", q=NQ) for r in range(2)]
        mixed = [wide[:, 20 * T + 512 * r:20 * T + 512 * r + 512].rearrange("p (q c) -> p q c", q=NQ) for r in range(2)]
        gel = block3(WORK + 4096, 4, T)
        std4 = block3(WORK + 4096, 4, T)
        silu_f = block3(WORK + 4096 + 4 * T, 2, T)
        xtok = block3(0, 3, D)
        acc = block3(3072, 3, D)
        silu_e = [ssm[:, 7168 + 512 * i:7680 + 512 * i] for i in range(2)]
        hid_e = [ssm[:, 8192 + 512 * i:8704 + 512 * i] for i in range(2)]
        y_e = ssm[:, 10240:11264]
        pick = block3(11264, 3, P)
        pickg = block3(11648, 3, P)
        logit_rows = ssm[:, 16000:16000 + T]
        spread = ssm[:, 12032:12032 + T]
        NR = MAXPASS + 1
        pos_of = block3(12800, 3, NR)
        sel_of = block3(12900, 3, NR)
        gate_of = block3(13000, 3, NR)
        lnb = block3(13312, 2, D)
        route = [block3(15400 + 24 * i, 3, NE) for i in range(9)]
        small3 = [ssm[:, 15700 + 4 * i:15703 + 4 * i] for i in range(16)]
        stats = block3(15800, 3, 12)
        mv = block3(15840, 3, 2)

        prm = r_all[0:96, 0:P]
        dtrow = r_all[0:96, P:P + 2]
        cols = r_all[0:C_END, 2 * P:3 * P]
        dsk = r_all[0:DEPTH * NG, 3 * P:3 * P + GC]
        iota_i = r_all[:, 4 * P:5 * P].bitcast(I32)
        rows = [spool[0:PSTATE, :], rows_d[:, :]]
        bank = [ctx.enter_context(nc.psum_tensor(f"bank{i}", [P, 512], F32)) for i in range(NBANK)]

        landed = [sem(f"weights_landed{i}") for i in range(RING)]
        used = sem("weights_used")
        filled = sem("tiles_filled")
        emptied = {"a": sem("tiles_emptied_by_act"), "d": sem("tiles_emptied_by_dve")}
        x_in, prm_in, cols_in, layer_in, router_in, lnb_in, stored = map(
            sem, ("x_in", "params_in", "columns_in", "layer_in", "router_in", "lnb_in", "stored"))
        pool_step, dve_step = sem("gpsimd_step"), sem("dve_step")
        const_ready, prm_rows, prm_ready = sem("constants_ready"), sem("prm_rows_ready"), sem("params_transposed")
        exp_arg, exp_ready, trig_arg, trig_ready = map(sem, ("exp_arg", "exp_ready", "trig_arg", "trig_ready"))
        vmat_ready, w1n_ready = sem("vmat_ready"), sem("w1n_ready")
        kern_ready, toep_zero, toep_ready, utok_zero = map(sem, ("kern_ready", "toep_zero", "toep_ready", "utok_zero"))
        udec_ready = sem("udec_ready")
        gelu_arg, gelu_tanh, y_ready, ob_ready, m_ready = map(
            sem, ("gelu_arg", "gelu_tanh", "y_ready", "ob_ready", "merged_ready"))
        centred, squared, std_ready, norm_ready, x_next = map(
            sem, ("centred", "squared", "std_ready", "norm_ready", "x_next"))
        rows_out, states_out = sem("rows_out"), sem("states_out")
        sel_ready, rexp_arg, rexp_ready, npass_ready = map(
            sem, ("sel_ready", "router_exp_arg", "router_exp_ready", "npass_ready"))
        pick_ready, pickg_ready = sem("pick_ready"), sem("pickg_ready")
        w_hi_ready, w_lo_ready = sem("w_hi_ready"), sem("w_lo_ready")
        xg_hi_ready, hidT_hi_ready, scatter_zero = map(sem, ("xg_hi_ready", "hidT_hi_ready", "scatter_zero"))
        fvar_ready, fstd_ready, y_out = sem("final_var"), sem("final_std"), sem("final_y")

        def tile_in(eng, key):
            eng.wait_ge(filled, tiles.filled[key])
            return bank[tiles.bank[key]]

        def wait_emptied(eng, key):
            owner, n = tiles.emptied[key]
            eng.wait_ge(emptied[owner], n)

        def pass_tile_in(eng, key, i):
            eng.wait_ge(filled, i * len(per_pass.keys) + (len(tiles.keys) + per_pass.filled[key]))
            return bank[pass_bank[key]]

        def wait_pass_emptied(eng, key, i, back=0):
            owner, n = per_pass.emptied[key]
            eng.wait_ge(emptied[owner],
                        i * per_pass.count[owner] + (tiles.count[owner] + n - back * per_pass.count[owner]))

        def landed_slot(eng, s, i):
            at = n_plan + s
            eng.wait_ge(landed[at % RING], i * (16 * PER_PASS // RING) + 16 * (at // RING + 1))
            return ring[at % RING]

        COLUMNS = ((C_BIN, "b_in", 48), (C_LN1G, "ln1_g", 16), (C_LN1B, "ln1_b", 16), (C_LN2G, "ln2_g", 8),
                   (C_LN2B, "ln2_b", 8), (C_PS, "pool_scale", 8), (C_BG, "b_glu", 8))

        def load_columns(eng, which, signal):
            for at, name, n in which:
                src = w[name].rearrange("l n -> (l n)").rearrange("(r n) -> r n", n=P)[0:n, :]
                eng.dma_start(cols[at:at + n, :], src).then_inc(signal, 16)

        LAYER_DMAS = 10

        def all_passes(eng):
            eng.wait_ge(npass_ready, 1)
            return eng.Fori(0, eng.value_load(npass_i[0:1, 0:1], min_val=NE, max_val=MAXPASS))

        block = ctx.enter_context(nc.Block())

        @block.sync
        def _(sp):
            for h in range(2):
                sp.dma_start(xstage[:, h, :],
                             w["x_prompt"][0].rearrange("(c j) n -> j c n", j=CHUNK)[4 * h:4 * h + 4]).then_inc(x_in, 16)
            sp.dma_start(xstage[0:NDEC, 2, :], w["x_sample"].rearrange("b o n -> (b o) n")).then_inc(x_in, 16)
            load_columns(sp, COLUMNS[2:], cols_in)
            for i, (key, src, k, n) in enumerate(plan):
                if i == 2:
                    sp.wait_ge(prm_in, 16 * 6)
                if i >= RING:
                    sp.wait_ge(used, i - RING + 1)
                sp.dma_start(ring[i % RING][:, 0:k * n].rearrange("p (k n) -> p k n", k=k), src)\
                    .then_inc(landed[i % RING], 16)

            def expert_weights(e, earlier):
                for s, (what, f, h) in enumerate(PASS_SLOTS):
                    i = (n_plan + s) % RING
                    if e is None and s < RING:
                        sp.wait_ge(used, n_plan + s - RING + 1)
                    else:
                        sp.wait_ge(w_lo_ready, earlier * PER_PASS + (s - RING + 1))
                    at = bass.ds(0 if e is None else e, 1)
                    if what == "down":
                        src = w["w_moe_down"][0][at, FCH * f + 256 * h:FCH * f + 256 * h + 256, :]
                    else:
                        src = w["w_moe_" + what][0][at, 512 * h:512 * h + 512, FCH * f:FCH * f + FCH]
                    k = src.shape[1] // P
                    sp.dma_start(ring[i][:, :].rearrange("p (k n) -> p k n", k=k),
                                 src.rearrange("a (k p) n -> p (a k) n", p=P)).then_inc(landed[i], 16)

            expert_weights(None, 0)
            with sp.Fori(1, NE) as e:
                expert_weights(e, e)
            sp.wait_ge(npass_ready, 1)
            npass = sp.value_load(npass_i[0:1, 0:1], min_val=NE, max_val=MAXPASS)
            for c in (1, 2):
                with sp.If(npass > c * NE):
                    with sp.Fori(0, NE) as e:
                        expert_weights(e, e + c * NE)

        @block.gpsimd
        def _(pool):
            n_step = 0

            def step(ins):
                nonlocal n_step
                n_step += 1
                ins.then_inc(pool_step, 1)
                pool.wait_ge(pool_step, n_step)

            def ready(ins):
                nonlocal n_const
                n_const += 1
                ins.then_inc(const_ready, 1)
                pool.wait_ge(const_ready, n_const)

            n_const = 0
            step(pool.memset(ident[:, :], 0.0))
            ready(pool.affine_select(out=ident[:, :], in_=ident[:, :], compare_op=ALU.not_equal, fill=1.0, base=0,
                                     pattern=[[-1, P]], channel_multiplier=1))
            step(pool.iota(iota_i[:, :], pattern=[[1, P]], base=0, channel_multiplier=0))
            ready(pool.tensor_copy(iota[:, :], iota_i[:, :]))
            ready(pool.memset(avg[:, :], 1.0 / D))
            ready(pool.memset(consts[:, 0:1], EPS))
            ready(pool.memset(consts[:, 1:2], math.pi / 2))
            pool.memset(utok[NCH:UC, :, :, :], 0.0).then_inc(utok_zero, 1)
            pool.wait_ge(utok_zero, 1)
            step(pool.memset(pmask[:, :, :], 1.0))
            step(pool.affine_select(out=pmask[:, :, :], in_=pmask[:, :, :], compare_op=ALU.is_ge, fill=0.0,
                                    base=PSTATE - 1, pattern=[[0, 4], [PSTATE, NDEC]], channel_multiplier=-1))
            for g, wd in enumerate(WINDOWS):
                ready(pool.affine_select(out=pmask[:, g, :], in_=pmask[:, g, :], compare_op=ALU.is_ge, fill=0.0,
                                         base=-(PSTATE + 1 - wd), pattern=[[-PSTATE, NDEC]], channel_multiplier=1))
            pool.memset(toep[:, :, :], 0.0).then_inc(toep_zero, 1)
            pool.wait_ge(toep_zero, 1)
            ready(pool.memset(ones[:, :], 1.0))
            step(pool.memset(tri[:, :], 1.0))
            ready(pool.affine_select(out=tri[:, :], in_=tri[:, :], compare_op=ALU.is_gt, fill=0.0, base=0,
                                     pattern=[[1, P]], channel_multiplier=-1))

            def toeplitz(l):
                pool.wait_ge(kern_ready, l + 1)
                if l == 0:
                    pool.wait_ge(toep_zero, 1)
                for j in range(CHUNK):
                    pool.dma_start(toep[GC * j:GC * j + GC, :, GC * j:P], kern[0:GC, :, 0:P - GC * j])\
                        .then_inc(toep_ready, 16)

            n_stored = 0
            for l in range(DEPTH):
                pool.dma_start(pool_s[l, :, 0:PSTATE - 1, :].rearrange("b r n -> b (r n)"),
                               w["state_pool"][l, :, 1:PSTATE, :].rearrange("b r n -> b (r n)")).then_inc(stored, 16)
                if l == 1:
                    toeplitz(l)
                    pool.wait_ge(toep_ready, 16 * CHUNK * 2)
                    pool.memset(utok[NCH:UC, :, :, :], 0.0).then_inc(utok_zero, 1)
                wait_emptied(pool, ("rows", l, 1))
                pool.dma_start(pool_p[l, 0], rows[0]).then_inc(rows_out, 16)
                pool.dma_start(pool_s[l, :, PSTATE - 1, :], rows[1]).then_inc(rows_out, 16)
                if l == 0:
                    toeplitz(l)
                wait_emptied(pool, ("stated", l))
                for r, (one, dec) in enumerate(((re_p, re_s), (im_p, im_s))):
                    pool.dma_start(one[l].rearrange("a g p -> (a g p)").rearrange("(q n) -> q n", n=P),
                                   srow_p[:, r, :]).then_inc(states_out, 16)
                    pool.dma_start(dec[l].rearrange("b g p -> (b g p)").rearrange("(q n) -> q n", n=P),
                                   srow[:, r, :]).then_inc(states_out, 16)
                n_stored += 1
            pool.wait_ge(x_next, 3 * KD)
            for i, name in enumerate(("ln2_g", "ln2_b")):
                pool.dma_start(lnb[:, i, :], w[name][DEPTH - 1].partition_broadcast(P)).then_inc(lnb_in, 16)
            for h, (_, m) in enumerate(TILES):
                pool.wait_ge(y_out, h + 1)
                if m == P:
                    for jl in range(4):
                        pool.dma_start(y_prompt[0].rearrange("(c j) n -> j c n", j=CHUNK)[4 * h + jl],
                                       acc[32 * jl:32 * jl + 32, h, :]).then_inc(stored, 16)
                        n_stored += 1
                else:
                    pool.dma_start(y_sample.rearrange("b o n -> (b o) n"), acc[0:m, h, :]).then_inc(stored, 16)
                    n_stored += 1
            pool.wait_ge(rows_out, 16 * 2 * DEPTH)
            pool.wait_ge(states_out, 16 * 4 * DEPTH)
            pool.wait_ge(stored, 16 * n_stored)

        @block.scalar
        def _(act):
            def load_layer(l):
                for r, (b, c, s) in enumerate((("b_re", "c_re", "state_ssm_re"), ("b_im", "c_im", "state_ssm_im"))):
                    act.dma_start(bnat[:, r, :, :], w[b][l].rearrange("(q h) p c -> (h p) q c", h=2)).then_inc(layer_in, 16)
                    for h in range(2):
                        act.dma_start(cnat[:, r, :, h, :], w[c][l].rearrange("(k g) c p -> (g c) k p", k=4))\
                            .then_inc(layer_in, 16)
                    act.dma_start(h0n[:, r, :], w[s][l].rearrange("b g p -> (b g p)").rearrange("(q n) -> q n", n=P))\
                        .then_inc(layer_in, 16)
                act.dma_start(spool[:, :], w["state_pool"][l].rearrange("b r n -> (b r) n")).then_inc(layer_in, 16)
                act.dma_start(ubias[:, :], w["b_in"][l, PW:PW + SW].partition_broadcast(P)).then_inc(layer_in, 16)

            act.dma_start(prm[0:32, :], w["lambda_re"].rearrange("l (q h) p -> (l q) (h p)", h=2)).then_inc(prm_in, 16)
            act.dma_start(prm[32:64, :], w["lambda_im"].rearrange("l (q h) p -> (l q) (h p)", h=2)).then_inc(prm_in, 16)
            act.dma_start(dtrow[64:96, :], w["log_dt"].rearrange("l (q h) -> (l q) h", h=2)).then_inc(prm_in, 16)
            load_columns(act, COLUMNS[:2], prm_in)
            act.dma_start(dsk[:, :], w["d_skip"].rearrange("l g c -> (l g) c")).then_inc(prm_in, 16)
            load_layer(0)
            act.dma_start(wrt[:, :, :], w["w_router"][0].rearrange("(k p) e -> p k e", p=P)).then_inc(router_in, 16)
            act.dma_start(brt[:, :], w["b_router"][0].partition_broadcast(P)).then_inc(router_in, 16)

            for k in range(0, KD, 2):
                act.activation(xT[:, k, :], tile_in(act, ("x", k))[:, 0:T], ACT.Copy).then_inc(emptied["a"], 1)

            act.wait_ge(prm_ready, 1)
            act.activation(tiny[:, 0, :], prmT[:, 64:96], ACT.Exp).then_inc(exp_ready, 1)
            act.wait_ge(exp_arg, 1)
            act.activation(tiny[:, 2, :], tiny[:, 1, :], ACT.Exp).then_inc(exp_ready, 1)
            act.wait_ge(trig_arg, 1)
            act.wait_ge(const_ready, 5)
            act.activation(tiny[:, 6, :], tiny[:, 4, :], ACT.Sin).then_inc(trig_ready, 1)
            act.activation(tiny[:, 7, :], tiny[:, 5, :], ACT.Sin, bias=consts[:, 1:2], scale=-1.0).then_inc(trig_ready, 1)

            def transposed_w1(l):
                for r in range(2):
                    for i in range(4):
                        act.activation(w1T[r][:, 4 * i:4 * i + 4, :],
                                       tile_in(act, ("w1t", l, r, i))[:, :].rearrange("p (q n) -> p q n", q=4),
                                       ACT.Copy).then_inc(emptied["a"], 1)

            def mixer(l):
                act.wait_ge(prm_ready, 3)
                for m in range(4):
                    ps = tile_in(act, ("ua", l, m))
                    bias = colT[:, C_BIN + 24 * l + m:C_BIN + 24 * l + m + 1]
                    act.activation(udec[:, m, :], ps[:, SEQ:T], ACT.Identity, bias=bias).then_inc(udec_ready, 1)
                    act.activation(pext[:, m, PAD:WX].rearrange("p (c j) -> p j c", j=CHUNK),
                                   ps[:, 0:SEQ].rearrange("p (j c) -> p j c", j=CHUNK), ACT.Identity, bias=bias)\
                        .then_inc(emptied["a"], 1)
                for i in range(3):
                    a, b = 12 * i, min(12 * i + 12, NG)
                    act.activation(ucol[:, a:b, :],
                                   tile_in(act, ("ut", l, i))[:, 0:(b - a) * UC].rearrange("p (g c) -> p g c", c=UC),
                                   ACT.Copy).then_inc(emptied["a"], 1)
                for m in range(16):
                    act.activation(gates[:, m, :], tile_in(act, ("gate", l, m))[:, 0:T], ACT.Tanh, scale=0.5,
                                   bias=colH[:, C_BIN + 24 * l + 8 + m:C_BIN + 24 * l + 9 + m]).then_inc(emptied["a"], 1)
                for r in range(2):
                    act.activation(sprev[r][:, :, NCH:UC],
                                   tile_in(act, ("h0", l, r))[:, 0:P].rearrange("p (b q) -> p q b", q=NQ),
                                   ACT.Copy).then_inc(emptied["a"], 1)
                for s in range(2):
                    n = (PSTATE, NDEC)[s]
                    act.activation(rows[s], tile_in(act, ("rows", l, s))[0:n, :], ACT.Copy).then_inc(emptied["a"], 1)
                if l == 0:
                    transposed_w1(l)
                for g in range(4):
                    act.activation(oaT[:, g, :], tile_in(act, ("mix", l, g))[:, 0:T], ACT.Copy,
                                   scale=colD[:, 4 * l + g:4 * l + g + 1]).then_inc(emptied["a"], 1)
                for i in range(0, NG // 4, 2):
                    to = ytok.rearrange("p j (q h) c -> p h j q c", h=2)[0:UC, 0, :, 2 * i:2 * i + 4, :]
                    act.activation(to,
                                   tile_in(act, ("y", l, i))[0:UC, :].rearrange("p (g j c) -> p j g c", g=4, j=CHUNK),
                                   ACT.Copy).then_inc(emptied["a"], 1)
                for k in range(4):
                    ps = tile_in(act, ("yt", l, k))
                    act.activation(yT[:, k, 0:SEQ], ps[:, 0:SEQ], ACT.Copy, scale=0.5)
                    act.activation(gel[:, k, 0:SEQ], ps[:, 0:SEQ], ACT.Square, scale=math.sqrt(0.044715)).then_inc(emptied["a"], 1)
                ps = tile_in(act, ("ytd", l))[:, 0:4 * NDEC].rearrange("p (k b) -> p k b", k=4)
                act.activation(yT[:, :, SEQ:T], ps, ACT.Copy, scale=0.5)
                act.activation(gel[:, :, SEQ:T], ps, ACT.Square, scale=math.sqrt(0.044715)).then_inc(emptied["a"], 1)
                if l == 1:
                    act.wait_ge(states_out, 16 * 4)
                act.activation(srow_p[:, :, :], tile_in(act, ("state", l))[0:NQ, 0:2 * P]
                               .rearrange("p (r n) -> p r n", r=2), ACT.Copy).then_inc(emptied["a"], 1)
                act.activation(srow[:, :, :], tile_in(act, ("stated", l))[:, 0:2 * P]
                               .rearrange("p (r n) -> p r n", r=2), ACT.Copy).then_inc(emptied["a"], 1)
                for k in range(4):
                    act.wait_ge(gelu_arg, 4 * l + k + 1)
                    act.activation(gel[:, k, :], gel[:, k, :], ACT.Tanh, scale=2.0 * math.sqrt(2.0 / math.pi))\
                        .then_inc(gelu_tanh, 1)
                act.wait_ge(y_ready, 4 * l + 4)
                for m in range(4):
                    act.activation(gel[:, m, :], tile_in(act, ("glu", l, m))[:, 0:T], ACT.Tanh, scale=0.5,
                                   bias=colH[:, C_BG + 4 * l + m:C_BG + 4 * l + m + 1]).then_inc(emptied["a"], 1)

            def layer_norm(l, which):
                n = 2 * l + which
                for h in range(4):
                    if h < 3:
                        act.wait_ge(centred, 3 * n + h + 1)
                    else:
                        wait_emptied(act, ("mean", l, which))
                    act.activation(mT[:, 2 * h:2 * h + 2, :], rT[:, 2 * h:2 * h + 2, :], ACT.Square).then_inc(squared, 1)
                act.activation(std4[:, 0, :], tile_in(act, ("var", l, which))[:, 0:T], ACT.Sqrt, bias=consts[:, 0:1])\
                    .then_inc(std_ready, 1)
                at = (C_LN1B + KD * l) if which == 0 else C_LN2B
                for k in range(KD):
                    act.wait_ge(norm_ready, KD * n + k + 1)
                    act.activation(xT[:, k, :], rT[:, k, :], ACT.Identity, bias=colT[:, at + k:at + k + 1])\
                        .then_inc(x_next, 1)

            def dense_ffn():
                act.wait_ge(rows_out, 16 * 2)
                load_layer(1)
                for f in range(NFT):
                    if f >= 2:
                        wait_emptied(act, ("fu", f - 2))
                    act.activation(silu_f[:, f % 2, :], tile_in(act, ("fg", f))[:, 0:T], ACT.Silu)\
                        .then_inc(emptied["a"], 1)
                transposed_w1(1)

            mixer(0)
            layer_norm(0, 0)
            dense_ffn()
            layer_norm(0, 1)
            mixer(1)
            layer_norm(1, 0)

            for i in range(6):
                h, half = i // 2, i % 2
                m = TILES[h][1]
                ps, at = tile_in(act, ("xtok", i)), slice(512 * half, 512 * half + 512)
                act.activation(xtok[0:m, h, at], ps[0:m, :], ACT.Copy).then_inc(emptied["a"], 1)
            act.wait_ge(rexp_arg, 1)
            act.activation(small3[3], small3[2], ACT.Exp).then_inc(rexp_ready, 1)
            wait_emptied(act, ("xtok", 5))
            for h, (_, m) in enumerate(TILES):
                act.activation(acc[0:m, h, :], xtok[0:m, h, :], ACT.Copy)
            def gathered_hi(ps, n):
                act.activation(xg_hi[:, 4 * n:4 * n + 4, :], ps[:, :].rearrange("p (k s) -> p k s", k=4), ACT.Copy)\
                    .then_inc(xg_hi_ready, 1)

            act.wait_ge(rows_out, 16 * 2 * DEPTH)
            for n in range(2):
                gathered_hi(tile_in(act, ("gather0", n)), n)

            def one_pass(i):
                def weights_hi(s):
                    ring_slot = landed_slot(act, s, i)
                    act.wait_ge(used, i * PER_PASS + (n_plan + s - PAIRS + 1))
                    act.activation(w_hi[s % PAIRS][:, :], ring_slot[:, :], ACT.Copy).then_inc(w_hi_ready, 1)

                def hidden_hi(f):
                    g = (f - 2) % NFC
                    act.wait_ge(used, i * PER_PASS + (n_plan + PASS_SLOTS.index(("down", g, 1)) + 1
                                                      - (PER_PASS if f < 2 else 0)))
                    act.activation(hidT_hi[f % 2][:, :, :], pass_tile_in(act, ("hT", f), i)[:, :]
                                   .rearrange("p (f s) -> p f s", f=4), ACT.Copy).then_inc(hidT_hi_ready, 1)

                for s, (what, f, h) in enumerate(PASS_SLOTS):
                    weights_hi(s)
                    if s < 2:
                        continue
                    what, f, h = PASS_SLOTS[s - 2]
                    if (what, h) == ("gate", 1):
                        wait_pass_emptied(act, ("u", (f - 2) % NFC), i, back=int(f < 2))
                        act.activation(silu_e[f % 2], pass_tile_in(act, ("g", f), i)[:, :], ACT.Silu)\
                            .then_inc(emptied["a"], 1)
                        if f == 0:
                            act.activation(spread, pass_tile_in(act, ("spread",), i)[:, 0:T], ACT.Copy)\
                                .then_inc(emptied["a"], 1)
                        else:
                            hidden_hi(f - 1)
                hidden_hi(NFC - 1)
                for n in range(2):
                    gathered_hi(pass_tile_in(act, ("gather", n), i), n)
                act.activation(y_e[:, 0:512], pass_tile_in(act, ("ye", 0), i)[:, :], ACT.Copy, scale=1.0 / ALPHA)\
                    .then_inc(emptied["a"], 1)

            with all_passes(act) as i:
                one_pass(i)
            act.wait_ge(fvar_ready, 1)
            act.activation(small3[11], small3[10], ACT.Sqrt).then_inc(fstd_ready, 1)

        @block.vector
        def _(dve):
            n_step = 0

            def step(ins):
                nonlocal n_step
                n_step += 1
                ins.then_inc(dve_step, 1)
                dve.wait_ge(dve_step, n_step)

            def tt(out, a, b, op):
                return dve.tensor_tensor(out, a, b, op)

            def complex_mul(out, a, b, t):
                tt(t[0], a[0], b[0], ALU.mult)
                step(tt(t[1], a[1], b[1], ALU.mult))
                step(tt(out[0], t[0], t[1], ALU.subtract))
                tt(t[0], a[0], b[1], ALU.mult)
                step(tt(t[1], a[1], b[0], ALU.mult))
                step(tt(out[1], t[0], t[1], ALU.add))

            def s5_columns(l, which):
                if 0 in which:
                    dve.wait_ge(layer_in, 16 * LAYER_DMAS * (l + 1))
                    if l == 1:
                        dve.wait_ge(toep_ready, 16 * CHUNK * 2)
                for h in which:
                    ps = tile_in(dve, ("ub", l, h))
                    if h < 2:
                        for jl in range(4):
                            q = slice(32 * jl, 32 * jl + 32)
                            ins = tt(utok[0:NCH, :, 4 * h + jl, :], ps[q, :].rearrange("p (g c) -> p g c", g=NG),
                                     ubias[q, :].rearrange("p (g c) -> p g c", g=NG), ALU.add)
                    else:
                        dve.wait_ge(utok_zero, l + 1)
                        for j in (0, CHUNK - 1):
                            ins = tt(utok[NCH:UC, :, j, :], ps[0:NDEC, :].rearrange("p (g c) -> p g c", g=NG),
                                     ubias[0:NDEC, :].rearrange("p (g c) -> p g c", g=NG), ALU.add)
                    ins.then_inc(emptied["d"], 1)

            (DT, ARE, MOD, AIM, RED, ABS, SIN, COS, LBR, LBI, FR, FI, UR, UI, MOD8, T0, T1, T2) = (
                tiny[:, i, :] for i in range(18))
            lre, lim = prmT[:, 0:32], prmT[:, 32:64]

            dve.wait_ge(prm_in, 16 * 6)
            dve.tensor_copy(prm[64:96, :].rearrange("p (h n) -> p h n", h=2),
                            dtrow[64:96, :].unsqueeze(2).to_broadcast([32, 2, NS])).then_inc(prm_rows, 1)
            for k in range(1, KD, 2):
                dve.tensor_copy(xT[:, k, :], tile_in(dve, ("x", k))[:, 0:T]).then_inc(emptied["d"], 1)
            ps = tile_in(dve, ("prm",))
            dve.tensor_copy(prmT[:, :], ps[:, 0:96]).then_inc(prm_ready, 1)
            dve.tensor_copy(dskT[:, :], ps[0:GC, 208:272]).then_inc(prm_ready, 1)
            step(dve.tensor_copy(colT[:, :], ps[:, 96:208]))
            dve.tensor_scalar(colH[:, :], colT[:, :], 0.5, None, ALU.mult).then_inc(prm_ready, 1)
            dve.tensor_scalar(colD[:, :], colT[:, C_PS:C_PS + 8], 2.0, None, ALU.mult).then_inc(emptied["d"], 1)

            def angles():
                dve.wait_ge(exp_ready, 1)
                tt(ARE, lre, DT, ALU.mult).then_inc(exp_arg, 1)
                step(tt(AIM, lim, DT, ALU.mult))
                step(dve.tensor_scalar(T0, AIM, 1.0 / (2.0 * math.pi), MAGIC, ALU.mult, ALU.add))
                step(dve.tensor_scalar(T0, T0, MAGIC, None, ALU.subtract))
                last = AIM
                for c in TWO_PI:
                    step(dve.scalar_tensor_tensor(out=RED, in0=T0, scalar=-c, in1=last, op0=ALU.mult, op1=ALU.add))
                    last = RED
                step(dve.tensor_scalar(RED, RED, PI_SAFE, -PI_SAFE, ALU.min, ALU.max))
                step(dve.tensor_scalar(T1, RED, -1.0, None, ALU.mult))
                tt(ABS, RED, T1, ALU.max).then_inc(trig_arg, 1)
                dve.wait_ge(exp_ready, 2)
                step(tt(T0, MOD, MOD, ALU.mult))
                step(tt(T0, T0, T0, ALU.mult))
                step(tt(MOD8, T0, T0, ALU.mult))
                dve.wait_ge(trig_ready, 2)
                complex_mul((UR, UI), (COS, SIN), (COS, SIN), (T0, T1))
                complex_mul((LBR, LBI), (UR, UI), (UR, UI), (T0, T1))
                complex_mul((UR, UI), (LBR, LBI), (LBR, LBI), (T0, T1))
                tt(LBR, MOD, COS, ALU.mult)
                tt(LBI, MOD, SIN, ALU.mult)
                tt(T0, lre, lre, ALU.mult)
                step(tt(T1, lim, lim, ALU.mult))
                step(tt(T0, T0, T1, ALU.add))
                step(dve.reciprocal(T0, T0))
                step(dve.tensor_scalar(T1, LBR, 1.0, None, ALU.subtract))
                tt(FR, T1, lre, ALU.mult)
                step(tt(T2, LBI, lim, ALU.mult))
                step(tt(FR, FR, T2, ALU.add))
                tt(FR, FR, T0, ALU.mult)
                tt(FI, LBI, lre, ALU.mult)
                step(tt(T2, T1, lim, ALU.mult))
                step(tt(FI, FI, T2, ALU.subtract))
                step(tt(FI, FI, T0, ALU.mult))

            def s5_tables(l):
                L = slice(NQ * l, NQ * l + NQ)

                def pair(tab, a, b):
                    return tab[:, 0, :, a:b], tab[:, 1, :, a:b]

                def wide_pair(p, n):
                    return tuple(x.to_broadcast([P, NQ, n]) for x in p)

                def work_pair(n):
                    return tuple(scr[:, r, 0:NQ * n].rearrange("p (q n) -> p q n", q=NQ) for r in range(2))

                for tab, first in ((powr, (LBR, LBI)), (turn, (UR, UI))):
                    dve.memset(tab[:, 0, :, 0:1], 1.0)
                    dve.memset(tab[:, 1, :, 0:1], 0.0)
                    dve.tensor_copy(tab[:, 0, :, 1:2], first[0][:, L].unsqueeze(2))
                    step(dve.tensor_copy(tab[:, 1, :, 1:2], first[1][:, L].unsqueeze(2)))
                n = 2
                while n < NPOW:
                    h = n // 2
                    complex_mul(pair(powr, h + 1, n + 1), pair(powr, 1, h + 1), wide_pair(pair(powr, h, h + 1), h),
                                work_pair(h))
                    n *= 2
                for j in range(CHUNK):
                    dve.tensor_copy(powv[:, :, :, j], powr[:, :, :, CHUNK - 1 - j])
                n = 2
                while n < NCH:
                    complex_mul(pair(turn, n, n + 1), pair(turn, n // 2, n // 2 + 1), pair(turn, n // 2, n // 2 + 1),
                                work_pair(1))
                    complex_mul(pair(turn, n + 1, 2 * n), pair(turn, 1, n), wide_pair(pair(turn, n, n + 1), n - 1),
                                work_pair(n - 1))
                    n *= 2
                dve.memset(decay[:, :, 0:1], 0.0)
                dve.tensor_copy(decay[:, :, 1:NCH], MOD8[:, L].unsqueeze(2).to_broadcast([P, NQ, NCH - 1]))
                dve.wait_ge(layer_in, 16 * LAYER_DMAS * (l + 1))
                complex_mul((bbar[:, 0, :, :], bbar[:, 1, :, :]),
                            tuple(x[:, L].unsqueeze(2).to_broadcast([P, NQ, GC]) for x in (FR, FI)),
                            (bnat[:, 0, :, :], bnat[:, 1, :, :]), work_pair(GC))

            def c_rows(l):
                for r in range(2):
                    ps = tile_in(dve, ("ct", l, r))[:, :].rearrange("p (q h c) -> p q h c", h=2, c=GC)
                    dve.tensor_copy(ctr[0:NS, r, :, :], ps[0:NS, :, 0, :])
                    dve.tensor_copy(ctr[NS:P, r, :, :], ps[NS:P, :, 1, :]).then_inc(emptied["d"], 1)

            def product(out, minus, powers, mat, n):
                pw = [powers[:, r, :, :].unsqueeze(3).to_broadcast([P, NQ, n, GC]) for r in range(2)]
                mt = [mat[:, r, :, :].unsqueeze(2).to_broadcast([P, NQ, n, GC]) for r in range(2)]
                t4 = prod[:, 0:NQ * n * GC].rearrange("p (q n c) -> p q n c", q=NQ, n=n)
                tt(out[0], pw[0], mt[0], ALU.mult)
                step(tt(t4, pw[1], mt[1], ALU.mult))
                step(tt(out[0], out[0], t4, ALU.subtract))
                tt(out[1], pw[0], mt[1], ALU.mult)
                step(tt(t4, pw[1], mt[0], ALU.mult))
                if not minus:
                    return tt(out[1], out[1], t4, ALU.add)
                flat = [x.rearrange("p q n c -> p (q n c)") for x in (out[1], t4)]
                return dve.scalar_tensor_tensor(out=flat[0], in0=flat[0], scalar=-1.0, in1=flat[1],
                                                op0=ALU.mult, op1=ALU.subtract)

            def s5_outputs(l):
                c_wait = tiles.emptied[("ct", l, 1)][1]
                dve.wait_ge(emptied["d"], c_wait)
                product(vmat, True, powr, ctr, NPOW).then_inc(vmat_ready, 1)
                dve.wait_ge(vmat_ready, l + 1)

            def s5_inputs(l):
                product(w1n, False, powv, bbar, CHUNK).then_inc(w1n_ready, 1)
                dve.wait_ge(w1n_ready, l + 1)

            def kernel_rows(l):
                for i in range(NG // 4):
                    to = kern.rearrange("p (q h) n -> p h q n", h=2)[0:GC, i % 2, 4 * (i // 2):4 * (i // 2) + 4, :]
                    dve.tensor_copy(to,
                                    tile_in(dve, ("kern", l, i))[0:GC, :].rearrange("p (g n) -> p g n", g=4))\
                        .then_inc(emptied["d"], 1)
                skip = scr[0:GC, :, :].rearrange("p r n -> p (r n)").rearrange("p (g c) -> p g c", g=NG)
                step(tt(skip, ident[0:GC, 0:GC].unsqueeze(1).to_broadcast([GC, NG, GC]),
                        dskT[:, NG * l:NG * l + NG].unsqueeze(2).to_broadcast([GC, NG, GC]), ALU.mult))
                wait_emptied(dve, ("kern", l, NG // 4 - 1))
                tt(kern[0:GC, :, 0:GC], kern[0:GC, :, 0:GC], skip, ALU.add).then_inc(kern_ready, 1)

            def pooling(l):
                step(dve.memset(pext[:, :, 0:PAD], 0.0))
                if l == 0:
                    dve.wait_ge(const_ready, 9)
                    for g, wd in enumerate(WINDOWS):
                        ins = dve.tensor_scalar(rcount[:, g, :], iota[:, 0:PAD], 1.0, float(wd), ALU.add, ALU.min)
                    step(ins)
                    step(dve.reciprocal(rcount[:, :, :], rcount[:, :, :]))
                wait_emptied(dve, ("ua", l, 3))
                step(tt(win_a[:, :, 1:WX], pext[:, :, 1:WX], pext[:, :, 0:WX - 1], ALU.add))
                step(tt(win_b[:, :, 3:WX], win_a[:, 1:4, 3:WX], win_a[:, 1:4, 1:WX - 2], ALU.add))
                step(tt(win_a[:, 2:4, 7:WX], win_b[:, 1:3, 7:WX], win_b[:, 1:3, 3:WX - 4], ALU.add))
                step(tt(win_b[:, 2, PSTATE:WX], win_a[:, 3, PSTATE:WX], win_a[:, 3, 7:WX - 8], ALU.add))
                sums = (win_a[:, 0, :], win_b[:, 0, :], win_a[:, 2, :], win_b[:, 2, :])
                step(tt(pdec[:, :, :], tile_in(dve, ("pd", l))[:, 0:4 * NDEC].rearrange("p (g b) -> p g b", g=4),
                        udec[:, :, :], ALU.add))
                for g, wd in enumerate(WINDOWS):
                    def steps(v, n):
                        return v.rearrange("p (c j) -> p c j", j=CHUNK)[:, 0:n, :]

                    out = poolT[:, g, 0:SEQ].rearrange("p (j c) -> p c j", j=CHUNK)
                    step(dve.scalar_tensor_tensor(out=out, in0=steps(sums[g][:, PAD:WX], NCH), scalar=1.0 / wd,
                                                  in1=steps(pext[:, g, PAD:WX], NCH), op0=ALU.mult, op1=ALU.subtract))
                    step(tt(pfix[:, :], sums[g][:, PAD:2 * PAD], rcount[:, g, :], ALU.mult))
                    tt(out[:, 0:2, :], steps(pfix[:, :], 2), steps(pext[:, g, PAD:2 * PAD], 2), ALU.subtract)
                    ins = dve.scalar_tensor_tensor(out=poolT[:, g, SEQ:T], in0=pdec[:, g, :], scalar=1.0 / wd,
                                                   in1=udec[:, g, :], op0=ALU.mult, op1=ALU.subtract)
                    if g < 3:
                        step(ins)
                    else:
                        ins.then_inc(emptied["d"], 1)

            def states(l):
                L = slice(NQ * l, NQ * l + NQ)
                er, ei = turn[:, 0, :, :], turn[:, 1, :, :]
                ar, ai, dec = (tile_in(dve, ("chunk", l, r)) for r in range(3))
                ar, ai = (x[:, :].rearrange("p (q c) -> p q c", q=NQ) for x in (ar, ai))
                tt(turned[0], er, ar, ALU.mult)
                tt(mixed[1], ei, ar, ALU.mult).then_inc(emptied["d"], 1)
                tt(turned[1], er, ai, ALU.mult)
                tt(mixed[0], ei, ai, ALU.mult).then_inc(emptied["d"], 1)
                wait_emptied(dve, ("chunk", l, 1))
                tt(turned[0], turned[0], mixed[0], ALU.add)
                step(tt(turned[1], turned[1], mixed[1], ALU.subtract))
                for r in range(2):
                    ins = dve.tensor_tensor_scan(mixed[r].rearrange("p q c -> p (q c)"),
                                                 decay[:, :, :].rearrange("p q c -> p (q c)"),
                                                 turned[r].rearrange("p q c -> p (q c)"), 0.0, ALU.mult, ALU.add)
                step(ins)
                for r, op in enumerate((ALU.subtract, ALU.add)):
                    tt(turned[0], er, mixed[r], ALU.mult)
                    step(tt(turned[1], ei, mixed[1 - r], ALU.mult))
                    dve.memset(sprev[r][:, :, 0:1], 0.0)
                    tt(sprev[r][:, :, 1:NCH], turned[0][:, :, 0:NCH - 1], turned[1][:, :, 0:NCH - 1], op)
                    step(tt(sfin[:, r, :].unsqueeze(2), turned[0][:, :, NCH - 1:NCH], turned[1][:, :, NCH - 1:NCH], op))
                wait_emptied(dve, ("h0", l, 1))
                h0 = [sprev[r][:, :, NCH:UC] for r in range(2)]
                lam = [x[:, L].unsqueeze(2).to_broadcast([P, NQ, NDEC]) for x in (LBR, LBI)]
                t = [scr[:, r, 0:NQ * NDEC].rearrange("p (q b) -> p q b", q=NQ) for r in range(2)]
                dec = dec[:, 0:2 * NQ * NDEC].rearrange("p (r q b) -> p r q b", r=2, q=NQ)
                for r, op in enumerate((ALU.subtract, ALU.add)):
                    tt(t[0], lam[0], h0[r], ALU.mult)
                    step(tt(t[1], lam[1], h0[1 - r], ALU.mult))
                    step(tt(t[0], t[0], t[1], op))
                    ins = tt(sfin_d[:, r, :, :].rearrange("p b q -> p q b"), t[0], dec[:, r, :, :], ALU.add)
                    if r == 0:
                        step(ins)
                ins.then_inc(emptied["d"], 1)

            def gelu(l):
                for k in range(4):
                    if k == 0:
                        wait_emptied(dve, ("ytd", l))
                    dve.scalar_tensor_tensor(out=gel[:, k, :], in0=gel[:, k, :], scalar=1.0, in1=yT[:, k, :],
                                             op0=ALU.add, op1=ALU.mult).then_inc(gelu_arg, 1)
                for k in range(4):
                    dve.wait_ge(gelu_tanh, 4 * l + k + 1)
                    dve.scalar_tensor_tensor(out=yT[:, k, :], in0=gel[:, k, :], scalar=1.0, in1=yT[:, k, :],
                                             op0=ALU.add, op1=ALU.mult).then_inc(y_ready, 1)

            def residual(key, factor):
                for m in range(KD):
                    dve.scalar_tensor_tensor(out=rT[:, m, :], in0=tile_in(dve, (*key, m))[:, 0:T], scalar=factor,
                                             in1=xT[:, m, :], op0=ALU.mult, op1=ALU.add).then_inc(emptied["d"], 1)

            def rsqrt(y, std, v, t):
                step(tt(t, y, y, ALU.mult))
                step(tt(t, t, v, ALU.mult))
                step(dve.tensor_scalar(t, t, -0.5, 1.5, ALU.mult, ALU.add))
                step(tt(y, y, t, ALU.mult))

            def layer_norm(l, which):
                n = 2 * l + which
                mean = tile_in(dve, ("mean", l, which))[:, 0:T].unsqueeze(1).to_broadcast([P, 2, T])
                wait_emptied(dve, ("out", l, KD - 1) if which == 0 else ("down", KD - 1))
                for k in range(0, KD, 2):
                    tt(rT[:, k:k + 2, :], mean, rT[:, k:k + 2, :], ALU.subtract)\
                        .then_inc(centred if k < KD - 2 else emptied["d"], 1)
                var = tile_in(dve, ("var", l, which))[:, 0:T]
                dve.wait_ge(std_ready, n + 1)
                t, y = std4[:, 1, :], std4[:, 2, :]
                step(dve.reciprocal(y, std4[:, 0, :]))
                step(tt(t, y, y, ALU.mult))
                dve.scalar_tensor_tensor(out=t, in0=var, scalar=EPS, in1=t, op0=ALU.add, op1=ALU.mult)\
                    .then_inc(emptied["d"], 1)
                wait_emptied(dve, ("var", l, which))
                step(dve.scalar_tensor_tensor(out=y, in0=t, scalar=3.0, in1=y, op0=ALU.subtract, op1=ALU.mult))
                at = (C_LN1G + KD * l) if which == 0 else C_LN2G
                for k in range(KD):
                    dve.scalar_tensor_tensor(out=rT[:, k, :], in0=rT[:, k, :], scalar=colH[:, at + k:at + k + 1],
                                             in1=y, op0=ALU.mult, op1=ALU.mult).then_inc(norm_ready, 1)

            def mixer(l):
                s5_columns(l, range(3))
                if l == 0:
                    c_rows(0)
                pooling(l)
                if l == 0:
                    s5_outputs(0)
                    s5_inputs(0)
                    kernel_rows(0)
                states(l)
                for m in range(KD):
                    wait_emptied(dve, ("gate", l, m))
                    dve.scalar_tensor_tensor(out=mT[:, m, :], in0=gates[:, m, :], scalar=1.0,
                                             in1=tile_in(dve, ("pa", l, m))[:, 0:T], op0=ALU.add, op1=ALU.mult)\
                        .then_inc(emptied["d"], 1)
                for i in range(1, NG // 4, 2):
                    to = ytok.rearrange("p j (q h) c -> p h j q c", h=2)[0:UC, 1, :, 2 * (i - 1):2 * (i - 1) + 4, :]
                    dve.tensor_copy(to,
                                    tile_in(dve, ("y", l, i))[0:UC, :].rearrange("p (g j c) -> p j g c", g=4, j=CHUNK))\
                        .then_inc(emptied["d"], 1)
                gelu(l)
                for m in range(4):
                    wait_emptied(dve, ("glu", l, m))
                    dve.scalar_tensor_tensor(out=gel[:, m, :], in0=gel[:, m, :], scalar=1.0, in1=yT[:, m, :],
                                             op0=ALU.add, op1=ALU.mult).then_inc(ob_ready, 1)
                for m in range(KD):
                    wait_emptied(dve, ("gate", l, 8 + m))
                    dve.scalar_tensor_tensor(out=gates[:, 8 + m, :], in0=gates[:, 8 + m, :], scalar=1.0,
                                             in1=tile_in(dve, ("pb", l, m))[:, 0:T], op0=ALU.add, op1=ALU.mult)\
                        .then_inc(emptied["d"], 1)
                    wait_emptied(dve, ("pb", l, m))
                    tt(mT[:, m, :], mT[:, m, :], gates[:, 8 + m, :], ALU.add).then_inc(m_ready, 1)
                residual(("out", l), 0.25 / ALPHA)
                layer_norm(l, 0)

            def dense_ffn():
                for f in range(NFT):
                    wait_emptied(dve, ("fg", f))
                    tt(hT[:, f, :], silu_f[:, f % 2, :], tile_in(dve, ("fu", f))[:, 0:T], ALU.mult)\
                        .then_inc(emptied["d"], 1)
                    if f == 3:
                        c_rows(1)
                    if f == 5:
                        s5_tables(1)
                    if f == 9:
                        s5_outputs(1)
                    if f == 14:
                        s5_inputs(1)
                kernel_rows(1)
                residual(("down",), 1.0 / ALPHA)
                layer_norm(0, 1)

            def slots(out, weight, i, ready):
                for h, (_, m) in enumerate(TILES):
                    ins = dve.tensor_scalar(out[0:m, h, :], iota[0:m, :], pos_of[0:m, h, bass.ds(i, 1)],
                                            weight[0:m, h, bass.ds(i, 1)], ALU.is_equal, ALU.mult)
                ins.then_inc(ready, 1)

            def routing():
                (LG, EQ, SC, BEST, SECOND, SEL, GATE, POS, WAY) = route
                (M1, M2, DIFF, EX, DEN, W1, W2, MX) = small3[0], small3[1], small3[2], small3[3], small3[4], small3[5], \
                    small3[6], small3[7]

                def over_e(v):
                    return v.unsqueeze(2).to_broadcast([P, 3, NE])

                dve.tensor_copy(logit_rows[0:NE, :], tile_in(dve, ("logit",))[0:NE, 0:T]).then_inc(emptied["d"], 1)
                step(dve.memset(LG, 0.0))
                dve.wait_ge(router_in, 32)
                dve.wait_ge(const_ready, 11)
                dve.tensor_scalar(WAY, iota[:, 0:NE].unsqueeze(1).to_broadcast([P, 3, NE]), -1.0, float(NE), ALU.mult, ALU.add)
                ps = tile_in(dve, ("logits",))
                tt(LG[:, 0:2, :], ps[:, 0:2 * NE].rearrange("p (h e) -> p h e", e=NE),
                   brt[:, :].unsqueeze(1).to_broadcast([P, 2, NE]), ALU.add)
                tt(LG[0:NDEC, 2, :], ps[0:NDEC, 2 * NE:3 * NE], brt[0:NDEC, :], ALU.add).then_inc(emptied["d"], 1)
                wait_emptied(dve, ("logits",))
                for m, one in ((M1, BEST), (M2, SECOND)):
                    step(dve.tensor_reduce(m, LG, AX.X, ALU.max))
                    step(tt(EQ, LG, over_e(m), ALU.is_equal))
                    step(tt(SC, EQ, WAY, ALU.mult))
                    step(dve.tensor_reduce(MX, SC, AX.X, ALU.max))
                    step(tt(one, SC, over_e(MX), ALU.is_equal))
                    if one is BEST:
                        step(dve.scalar_tensor_tensor(out=LG, in0=BEST, scalar=-3.0e38, in1=LG, op0=ALU.mult, op1=ALU.add))
                tt(SEL, BEST, SECOND, ALU.add).then_inc(sel_ready, 1)
                tt(DIFF, M2, M1, ALU.subtract).then_inc(rexp_arg, 1)
                dve.memset(pos_of, -1.0)
                dve.memset(gate_of, 0.0)
                dve.memset(POS, 0.0)
                step(dve.memset(sel_of, 0.0))
                rounds = [slice(NE * c, NE * c + NE) for c in range(3)]
                for at in rounds:
                    dve.tensor_copy(sel_of[:, :, at], SEL)
                ps = tile_in(dve, ("pos",))
                dve.tensor_copy(POS[:, 0:2, :], ps[:, 0:2 * NE].rearrange("p (h e) -> p h e", e=NE))
                dve.tensor_copy(POS[0:NDEC, 2, :], ps[0:NDEC, 2 * NE:3 * NE])
                dve.tensor_reduce(MX[:, 0:1], ps[:, 3 * NE:4 * NE], AX.X, ALU.max).then_inc(emptied["d"], 1)
                wait_emptied(dve, ("pos",))
                for c, at in enumerate(rounds):
                    ins = dve.tensor_scalar(pos_of[:, :, at], POS, float(-P * c), None, ALU.add)
                step(ins)
                slots(pick, sel_of, 0, pick_ready)
                step(dve.tensor_scalar(DEN[:, 0:1], MX[:, 0:1], float(P), float(NE), ALU.is_gt, ALU.mult))
                step(dve.tensor_scalar(DEN[:, 1:2], MX[:, 0:1], float(2 * P), float(NE), ALU.is_gt, ALU.mult))
                step(tt(DEN[:, 0:1], DEN[:, 0:1], DEN[:, 1:2], ALU.add))
                dve.tensor_scalar(npass_i[0:1, 0:1], DEN[0:1, 0:1], float(NE), None, ALU.add).then_inc(npass_ready, 1)
                dve.wait_ge(npass_ready, 1)
                dve.wait_ge(rexp_ready, 1)
                step(dve.tensor_scalar(DEN, EX, 1.0, None, ALU.add))
                step(dve.reciprocal(W1, DEN))
                step(tt(W2, EX, W1, ALU.mult))
                tt(BEST, BEST, over_e(W1), ALU.mult)
                step(tt(SECOND, SECOND, over_e(W2), ALU.mult))
                step(tt(GATE, BEST, SECOND, ALU.add))
                for at in rounds:
                    dve.tensor_copy(gate_of[:, :, at], GATE)
                dve.memset(spread, 0.0)
                dve.memset(y_e, 0.0).then_inc(scatter_zero, 1)

            def gathered_lo(ps, n, count):
                dve.wait_ge(xg_hi_ready, count)
                at = slice(4 * n, 4 * n + 4)
                tt(xg_lo[:, at, :], ps[:, :].rearrange("p (k s) -> p k s", k=4), xg_hi[:, at, :], ALU.subtract)\
                    .then_inc(emptied["d"], 1)

            def scattered(i, steps):
                for s in steps:
                    h, half = s % 3, s // 3
                    m = TILES[h][1]
                    part_ = acc[0:m, h, 512 * half:512 * half + 512]
                    tt(part_, part_, pass_tile_in(dve, ("scatter", s), i)[0:m, :], ALU.add).then_inc(emptied["d"], 1)

            def one_pass(i):
                def hidden_lo(f):
                    dve.wait_ge(hidT_hi_ready, i * NFC + (f + 1))
                    tt(hidT_lo[f % 2][:, :, :], pass_tile_in(dve, ("hT", f), i)[:, :]
                       .rearrange("p (f s) -> p f s", f=4), hidT_hi[f % 2][:, :, :], ALU.subtract)\
                        .then_inc(emptied["d"], 1)

                for s in range(PER_PASS):
                    dve.wait_ge(w_hi_ready, i * PER_PASS + (s + 1))
                    tt(w_lo[s % PAIRS][:, :], ring[(n_plan + s) % RING][:, :], w_hi[s % PAIRS][:, :], ALU.subtract)\
                        .then_inc(w_lo_ready, 1)
                    if s < 3:
                        scattered(i, (2 * s, 2 * s + 1))
                    if s == 1:
                        wait_pass_emptied(dve, ("spread",), i, back=1)
                        slots(pickg, gate_of, i, pickg_ready)
                    if s < 2:
                        continue
                    what, f, h = PASS_SLOTS[s - 2]
                    if (what, h) == ("gate", 1) and f > 0:
                        hidden_lo(f - 1)
                    if (what, h) == ("up", 1):
                        wait_pass_emptied(dve, ("g", f), i)
                        wait_pass_emptied(dve, ("hT", (f - 2) % NFC), i, back=int(f < 2))
                        tt(hid_e[f % 2], silu_e[f % 2], pass_tile_in(dve, ("u", f), i)[:, :], ALU.mult)\
                            .then_inc(emptied["d"], 1)
                        if f == 2:
                            slots(pick, sel_of, i + 1, pick_ready)
                hidden_lo(NFC - 1)
                for n in range(2):
                    gathered_lo(pass_tile_in(dve, ("gather", n), i), n, i * 2 + (n + 3))
                dve.tensor_scalar(y_e[:, 512:1024], pass_tile_in(dve, ("ye", 1), i)[:, :], 1.0 / ALPHA, None, ALU.mult)\
                    .then_inc(emptied["d"], 1)

            def final_norm(n_done):
                VAR, STD, Y, TMP = small3[10], small3[11], small3[12], small3[13]
                dve.wait_ge(emptied["d"], n_done)
                step(dve.memset(mv, 1.0))
                for h, (_, m) in enumerate(TILES):
                    for half in range(2):
                        ins = dve.bn_stats(stats[0:m, h, 6 * half:6 * half + 6], acc[0:m, h, 512 * half:512 * half + 512])
                    step(ins)
                    step(dve.bn_aggr(mv[0:m, h, :], stats[0:m, h, :]))
                dve.tensor_scalar(VAR, mv[:, :, 1], EPS, None, ALU.add).then_inc(fvar_ready, 1)
                dve.wait_ge(fstd_ready, 1)
                step(dve.reciprocal(Y, STD))
                rsqrt(Y, None, VAR, TMP)
                dve.wait_ge(lnb_in, 32)
                for h, (_, m) in enumerate(TILES):
                    row = acc[0:m, h, :]
                    step(dve.tensor_scalar(row, row, mv[0:m, h, 0:1], Y[0:m, h:h + 1], ALU.subtract, ALU.mult))
                    step(tt(row, row, lnb[0:m, 0, :], ALU.mult))
                    tt(row, row, lnb[0:m, 1, :], ALU.add).then_inc(y_out, 1)

            angles()
            s5_tables(0)
            mixer(0)
            dense_ffn()
            mixer(1)
            routing()
            gathered_lo(tile_in(dve, ("gather0", 0)), 0, 1)
            gathered_lo(tile_in(dve, ("gather0", 1)), 1, 2)
            dve.wait_ge(npass_ready, 1)
            npass = dve.value_load(npass_i[0:1, 0:1], min_val=NE, max_val=MAXPASS)
            with dve.Fori(0, npass) as i:
                one_pass(i)
            scattered(npass, range(6))
            final_norm(npass * per_pass.count["d"] + (tiles.count["d"] + 6))

        @block.tensor
        def _(pe):
            owed = [0]

            def mm(out, lhsT, rhs, start, stop, signal=None):
                ins = pe.matmul(out, lhsT, rhs, start=start, stop=stop, skip_group_check=True)
                if signal is not None:
                    ins.then_inc(signal, 1)
                elif owed[0]:
                    ins.then_inc(used, 1)
                    owed[0] = 0
                return ins

            def turn_over(out, in_, n, signal=None, at=0):
                ins = pe.transpose(out, in_, ident[at:at + n, at:at + n])
                if signal is not None:
                    ins.then_inc(signal, 1)
                elif owed[0]:
                    ins.then_inc(used, 1)
                    owed[0] = 0

            def claim(key):
                i = tiles.filled[key] - 1
                if i >= NBANK:
                    wait_emptied(pe, tiles.keys[i - NBANK])
                return bank[tiles.bank[key]]

            def slot(key):
                i = slot_of[key]
                _, _, k, n = plan[i]
                pe.wait_ge(landed[i % RING], 16 * (i // RING + 1))
                return ring[i % RING][:, 0:k * n].rearrange("p (k n) -> p k n", k=k)

            def through(signal_given):
                if signal_given is None:
                    return used
                assert not owed[0]
                owed[0] = 1
                return signal_given

            def project(names, slots_, rhs, ready=None):
                for m, name in enumerate(names):
                    ps = claim(name)
                    k = 0
                    n_k = sum(plan[slot_of[s]][2] for s in slots_)
                    for s in slots_:
                        wt = slot(s)
                        for kk in range(wt.shape[1]):
                            if ready and m == 0:
                                ready(k)
                            end_tile, end_slot = k == n_k - 1, kk == wt.shape[1] - 1 and m == len(names) - 1
                            sig = filled if end_tile else None
                            if end_slot:
                                sig = through(sig)
                            mm(ps[:, 0:T], wt[:, kk, P * m:P * m + P], rhs[:, k, :], k == 0, end_tile, sig)
                            k += 1

            def stream(l):
                if l == 0:
                    return lambda k: wait_emptied(pe, ("x", k))
                return lambda k: pe.wait_ge(x_next, KD + k + 1)

            def c_transposed(l):
                pe.wait_ge(layer_in, 16 * LAYER_DMAS * (l + 1))
                for r in range(2):
                    ps = claim(("ct", l, r))
                    for k in range(4):
                        turn_over(ps[:, P * k:P * k + P], cnat[:, r, k, :, :], P, filled if k == 3 else None)

            def s5_matrices(l):
                pe.wait_ge(w1n_ready, l + 1)
                for r in range(2):
                    for i in range(4):
                        ps = claim(("w1t", l, r, i))
                        for q in range(4):
                            turn_over(ps[:, P * q:P * q + P], w1n[r][:, 4 * i + q, :, :], P, filled if q == 3 else None)
                pe.wait_ge(vmat_ready, l + 1)
                for i in range(NG // 4):
                    ps = claim(("kern", l, i))
                    at = NS * (i % 2)
                    for n in range(4):
                        q = 4 * (i // 2) + n
                        for r in range(2):
                            mm(ps[0:GC, P * n:P * n + P], bbar[at:at + NS, r, q, :],
                               vmat[r][at:at + NS, q, 0:CHUNK, :], r == 0, r == 1, filled if n == 3 and r == 1 else None)

            def parameters():
                pe.wait_ge(prm_in, 16 * 6)
                pe.wait_ge(cols_in, 16 * 5)
                pe.wait_ge(prm_rows, 1)
                ps = claim(("prm",))
                turn_over(ps[:, 0:96], prm, 96)
                turn_over(ps[:, 96:208], cols, C_END)
                turn_over(ps[0:GC, 208:272], dsk, DEPTH * NG, filled)

            def mixer(l):
                for h, (at, m) in enumerate(TILES):
                    if l == 0 and h == 0:
                        parameters()
                    ps = claim(("ub", l, h))
                    for k in range(KD):
                        if h == 0:
                            stream(l)(k)
                        wt = slot(("ub", l, k // 4))
                        sig = filled if k == KD - 1 else None
                        if h == 2 and k % 4 == 3:
                            sig = through(sig)
                        mm(ps[0:m, :], xT[:, k, at:at + m], wt[:, k % 4, :], k == 0, k == KD - 1, sig)
                project([("ua", l, m) for m in range(4)], [("ua", l, h) for h in range(2)], xT)
                if l == 0:
                    c_transposed(0)
                wait_emptied(pe, ("ub", l, 2))
                for i in range(3):
                    ps = claim(("ut", l, i))
                    a, b = 12 * i, min(12 * i + 12, NG)
                    for g in range(a, b):
                        turn_over(ps[:, UC * (g - a):UC * (g - a) + UC], utok[0:UC, g, :, :], UC,
                                  filled if g == b - 1 else None)
                pe.wait_ge(layer_in, 16 * LAYER_DMAS * (l + 1))
                pe.wait_ge(const_ready, 9)
                ps = claim(("pd", l))
                for g in range(4):
                    mm(ps[:, NDEC * g:NDEC * g + NDEC], spool[:, P * g:P * g + P], pmask[:, g, :], True, True,
                       filled if g == 3 else None)
                for n in range(4):
                    project([("gate", l, 4 * n + m) for m in range(4)], [("gate", l, n, h) for h in range(2)], xT)
                for r in range(2):
                    turn_over(claim(("h0", l, r))[:, 0:P], h0n[:, r, :], P, filled)
                wait_emptied(pe, ("ua", l, 3))
                ps = claim(("rows", l, 0))
                for g in range(4):
                    turn_over(ps[0:PSTATE, P * g:P * g + P], pext[:, g, WX - PSTATE:WX], P, filled if g == 3 else None)
                ps = claim(("rows", l, 1))
                for g in range(4):
                    turn_over(ps[0:NDEC, P * g:P * g + P], udec[:, g, :], P, filled if g == 3 else None)
                if l == 0:
                    s5_matrices(0)
                wait_emptied(pe, ("w1t", l, 1, 3))
                wait_emptied(pe, ("ut", l, 2))
                for r in range(2):
                    ps = claim(("chunk", l, r))
                    for g in range(NG):
                        q, at = g // 2, NS * (g % 2)
                        mm(ps[at:at + NS, NCH * q:NCH * q + NCH], w1T[r][:, q, at:at + NS], ucol[:, g, 0:NCH],
                           True, True, filled if g == NG - 1 else None)
                ps = claim(("chunk", l, 2))
                for r in range(2):
                    for g in range(NG):
                        q, at = g // 2, NS * (g % 2)
                        c = NDEC * (NQ * r + q)
                        mm(ps[at:at + NS, c:c + NDEC], w1T[r][P - 32:P, q, at:at + NS], ucol[P - 32:P, g, NCH:UC],
                           True, True, filled if r == 1 and g == NG - 1 else None)
                wait_emptied(pe, ("pd", l))
                wt = slot(("wpool", l))
                for g in range(4):
                    sig = through(filled) if g == 3 else filled
                    mm(claim(("mix", l, g))[:, 0:T], wt[:, g, :], poolT[:, g, :], True, True, sig)
                for h in range(2):
                    project([("pa", l, 4 * h + m) for m in range(4)], [("pa", l, h)], oaT,
                            lambda k: wait_emptied(pe, ("mix", l, k)))
                pe.wait_ge(toep_ready, 16 * CHUNK * (l + 1))
                wait_emptied(pe, ("chunk", l, 2))
                for i in range(NG // 4):
                    ps = claim(("y", l, i))
                    half = i % 2
                    at = NS * half
                    qs = range(4 * (i // 2), 4 * (i // 2) + 4)
                    for n, q in enumerate(qs):
                        mm(ps[0:UC, P * n:P * n + P], ucol[:, 2 * q + half, :], toep[:, 2 * q + half, :], n == 0, False)
                    for n, q in enumerate(qs):
                        for r in range(2):
                            mm(ps[0:UC, P * n:P * n + P], sprev[r][at:at + NS, q, :], vmat[r][at:at + NS, q, 1:NPOW, :],
                               False, n == 3 and r == 1, filled if n == 3 and r == 1 else None)
                wait_emptied(pe, ("y", l, NG // 4 - 2))
                wait_emptied(pe, ("y", l, NG // 4 - 1))
                for k in range(4):
                    ps = claim(("yt", l, k))
                    for j in range(CHUNK):
                        turn_over(ps[:, NCH * j:NCH * j + NCH], ytok[0:NCH, j, 8 * k:8 * k + 8, :], NCH,
                                  filled if j == CHUNK - 1 else None)
                ps = claim(("ytd", l))
                for k in range(4):
                    turn_over(ps[:, NDEC * k:NDEC * k + NDEC], ytok[NCH:UC, 0, 8 * k:8 * k + 8, :], NDEC,
                              filled if k == 3 else None, NCH)
                ps = claim(("state", l))
                for r in range(2):
                    turn_over(ps[0:NQ, P * r:P * r + P], sfin[:, r, :], P, filled if r else None)
                ps = claim(("stated", l))
                for r in range(2):
                    turn_over(ps[:, P * r:P * r + P], sfin_d[:, r, :, :], P,
                              filled if r else None)
                keep_warm(("yt", l, 3), 6)
                project([("glu", l, m) for m in range(4)], [("glu", l)], yT, lambda k: pe.wait_ge(y_ready, 4 * l + k + 1))
                for h in range(2):
                    project([("pb", l, 4 * h + m) for m in range(4)], [("pb", l, h)], gel,
                            lambda k: pe.wait_ge(ob_ready, 4 * l + k + 1))
                for n in range(4):
                    project([("out", l, 2 * n + m) for m in range(2)], [("out", l, n)], mT,
                            lambda k: pe.wait_ge(m_ready, KD * l + k + 1))
                layer_norm(l, 0)

            def keep_warm(key, n):
                wait_emptied(pe, key)
                for _ in range(n):
                    mm(bank[tiles.bank[key]][:, 0:P], ident[:, :], ident[:, :], True, True)

            def layer_norm(l, which):
                n = 2 * l + which
                ps = claim(("mean", l, which))
                for k in range(KD):
                    wait_emptied(pe, ("out", l, k) if which == 0 else ("down", k))
                    mm(ps[:, 0:T], avg[:, :], rT[:, k, :], k == 0, k == KD - 1, filled if k == KD - 1 else None)
                ps = claim(("var", l, which))
                for k in range(KD):
                    pe.wait_ge(squared, 4 * n + k // 2 + 1)
                    mm(ps[:, 0:T], avg[:, :], mT[:, k, :], k == 0, k == KD - 1, filled if k == KD - 1 else None)
                keep_warm(("mean", l, which), 18)

            def dense_ffn():
                for c in range(NFT // 2):
                    for m in range(2):
                        f = 2 * c + m
                        for name, s in (("fg", "w_ffn_gate"), ("fu", "w_ffn_up")):
                            ps = claim((name, f))
                            wt = slot((s, c))
                            for k in range(KD):
                                if f == 0:
                                    pe.wait_ge(x_next, k + 1)
                                sig = filled if k == KD - 1 else None
                                if k == KD - 1 and m == 1:
                                    sig = through(sig)
                                mm(ps[:, 0:T], wt[:, k, P * m:P * m + P], xT[:, k, :], k == 0, k == KD - 1, sig)
                        if f == 3:
                            c_transposed(1)
                s5_matrices(1)
                for n in range(4):
                    ps = [claim(("down", 2 * n + m)) for m in range(2)]
                    for a in range(0, NFT, 8):
                        wt = slot(("down", n, a))
                        for m in range(2):
                            for kk in range(wt.shape[1]):
                                f = a + kk
                                if n == 0 and m == 0:
                                    wait_emptied(pe, ("fu", f))
                                sig = filled if f == NFT - 1 else None
                                if m == 1 and kk == wt.shape[1] - 1:
                                    sig = through(sig)
                                mm(ps[m][:, 0:T], wt[:, kk, P * m:P * m + P], hT[:, f, :], f == 0, f == NFT - 1, sig)
                layer_norm(0, 1)

            pe.wait_ge(const_ready, 1)
            pe.wait_ge(x_in, 16 * 3)
            for k in range(KD):
                ps = claim(("x", k))
                for h, (at, m) in enumerate(TILES):
                    turn_over(ps[:, at:at + m], xstage[0:m, h, P * k:P * k + P], m, filled if h == 2 else None)
            mixer(0)
            dense_ffn()
            mixer(1)

            pe.wait_ge(router_in, 32)
            ps = claim(("logit",))
            for k in range(KD):
                pe.wait_ge(x_next, 2 * KD + k + 1)
                mm(ps[0:NE, 0:T], wrt[:, k, :], xT[:, k, :], k == 0, k == KD - 1, filled if k == KD - 1 else None)
            wait_emptied(pe, ("logit",))
            ps = claim(("logits",))
            for h, (at, m) in enumerate(TILES):
                turn_over(ps[0:m, NE * h:NE * h + NE], logit_rows[0:NE, at:at + m], NE, filled if h == 2 else None)
            for i in range(6):
                h, half = i // 2, i % 2
                at, m = TILES[h]
                ps = claim(("xtok", i))
                for kk in range(4):
                    turn_over(ps[0:m, P * kk:P * kk + P], xT[:, 4 * half + kk, at:at + m], P, filled if kk == 3 else None)
            pe.wait_ge(sel_ready, 1)
            pe.wait_ge(const_ready, 11)
            ps = claim(("pos",))
            for h in range(4):
                m = TILES[h][1] if h < 3 else P
                for hh in range(min(h + 1, 3)):
                    mk = TILES[hh][1]
                    mat = tri if hh == h else ones
                    mm(ps[0:m, NE * h:NE * h + NE], mat[0:mk, 0:m], route[5][0:mk, hh, :], hh == 0, hh == min(h, 2),
                       filled if h == 3 and hh == 2 else None)

            def gather_tile(ps, n):
                for kk in range(4):
                    k = 4 * n + kk
                    for h, (_, m) in enumerate(TILES):
                        mm(ps[:, P * kk:P * kk + P], xtok[0:m, h, P * k:P * k + P], pick[0:m, h, :],
                           h == 0, h == 2, filled if kk == 3 and h == 2 else None)

            keep_warm(("xtok", 5), 8)
            pe.wait_ge(pick_ready, 1)
            for n in range(2):
                gather_tile(claim(("gather0", n)), n)
            keep_warm(("xtok", 5), 10)
            for owner in "ad":
                pe.wait_ge(emptied[owner], tiles.count[owner])
            pe.wait_ge(scatter_zero, 1)

            def claim_in_pass(key, i):
                b = pass_bank[key]
                same = [k for k in per_pass.keys if pass_bank[k] == b]
                at = same.index(key)
                wait_pass_emptied(pe, same[at - 1], i, back=int(at == 0))
                return bank[b]

            def split_slot(what, f, h, i):
                s = PASS_SLOTS.index((what, f, h))
                pe.wait_ge(w_lo_ready, i * PER_PASS + (s + 1))
                k = 2 if what == "down" else 4
                return [v[s % PAIRS][:, :].rearrange("p (k n) -> p k n", k=k) for v in (w_hi, w_lo)]

            def mm_split(out, x, wt, start, stop, signal, ends_slot):
                mm(out, x[0], wt[0], start, False)
                mm(out, x[0], wt[1], False, False)
                mm(out, x[1], wt[0], False, stop, through(signal) if ends_slot else signal)

            def scatter(i):
                for s in range(6):
                    h, half = s % 3, s // 3
                    at, m = TILES[h]
                    if h == 0:
                        wait_pass_emptied(pe, ("ye", half), i, back=1)
                    ps = claim_in_pass(("scatter", s), i)
                    mm(ps[0:m, :], spread[:, at:at + m], y_e[:, 512 * half:512 * half + 512], True, True, filled)

            def one_pass(i):
                def products(name, f):
                    what = {"g": "gate", "u": "up"}[name]
                    ps = claim_in_pass((name, f), i)
                    for h in range(2):
                        wt = split_slot(what, f, h, i)
                        for kk in range(4):
                            k = 4 * h + kk
                            mm_split(ps[:, :], (xg_hi[:, k, :], xg_lo[:, k, :]), (wt[0][:, kk, :], wt[1][:, kk, :]),
                                     k == 0, k == KD - 1, filled if k == KD - 1 else None, kk == 3)

                def hidden_transposed(f):
                    wait_pass_emptied(pe, ("u", f), i)
                    ps = claim_in_pass(("hT", f), i)
                    for n in range(4):
                        turn_over(ps[:, P * n:P * n + P], hid_e[f % 2][:, P * n:P * n + P], P, filled if n == 3 else None)

                def down(f):
                    if f == 0:
                        for n in range(2):
                            claim_in_pass(("ye", n), i)
                    wait_pass_emptied(pe, ("hT", f), i)
                    steps = [(h, kk, n) for h in range(2) for kk in range(2) for n in range(2)]
                    if f == NFC - 1:
                        steps = [(h, kk, n) for n in range(2) for h in range(2) for kk in range(2)]
                    wt = [None, None]
                    for h, kk, n in steps:
                        if wt[h] is None:
                            wt[h] = split_slot("down", f, h, i)
                        k = 2 * h + kk
                        end = f == NFC - 1 and k == 3
                        mm_split(bank[4 + n][:, :], (hidT_hi[f % 2][:, k, :], hidT_lo[f % 2][:, k, :]),
                                 [v[:, kk, 512 * n:512 * n + 512] for v in wt[h]], f == 0 and k == 0, end,
                                 filled if end else None, kk == 1 and n == 1)

                scatter(i)
                wait_pass_emptied(pe, ("gather", 1), i, back=1)
                for f in range(NFC):
                    products("g", f)
                    if f == 0:
                        pe.wait_ge(pickg_ready, i + 1)
                        ps = claim_in_pass(("spread",), i)
                        for h, (at, m) in enumerate(TILES):
                            turn_over(ps[:, at:at + m], pickg[0:m, h, :], m, filled if h == 2 else None)
                    else:
                        hidden_transposed(f - 1)
                    products("u", f)
                    if f > 0:
                        down(f - 1)
                hidden_transposed(NFC - 1)
                pe.wait_ge(pick_ready, i + 2)
                for n in range(2):
                    gather_tile(claim_in_pass(("gather", n), i), n)
                down(NFC - 1)
                mm(bank[pass_bank[("scatter", 0)]][0:1, 0:1], ident[0:1, 0:1], ident[0:1, 0:1], True, True)
                assert not owed[0]

            pe.wait_ge(npass_ready, 1)
            npass = pe.value_load(npass_i[0:1, 0:1], min_val=NE, max_val=MAXPASS)
            with pe.Fori(0, npass) as i:
                one_pass(i)
            scatter(npass)


_OUTS = [(1, SEQ, D), (NDEC, 1, D), (DEPTH, 1, PSTATE, PW), (DEPTH, 1, NG, NS), (DEPTH, 1, NG, NS),
         (DEPTH, NDEC, PSTATE, PW), (DEPTH, NDEC, NG, NS), (DEPTH, NDEC, NG, NS)]


def kernel(**inputs):
    import numpy as _np
    import concourse.bacc as _bacc
    from concourse.bass_utils import run_bass_kernel_spmd as _run

    nc = _bacc.Bacc("TRN2", target_bir_lowering=False, num_devices=1)
    arrays, args = {}, {}
    for name, x in inputs.items():
        a = _np.ascontiguousarray(x)
        arrays[f"in_{name}_dram"] = a
        args[name] = nc.dram_tensor(f"in_{name}_dram", a.shape, F32, kind="ExternalInput").ap()
    outs = [nc.dram_tensor(f"out_{i}_dram", s, F32, kind="ExternalOutput").ap() for i, s in enumerate(_OUTS)]
    trunk_kernel(nc, args, outs)
    r = _run(nc, [arrays], core_ids=[0])
    return tuple(r.results[0][f"out_{i}_dram"] for i in range(len(_OUTS)))
```
